# Optimizing a Trainium2 kernel written in Bass

```python
import jax, jax.numpy as jnp
from jax import lax
import numpy as np

D_MODEL = 1024
BATCH = 1
SEQ = 512
DEPTH = 2
DEC_BATCH = 1
DEC_SEQ = 64
PAST_LEN = 128

CHUNK = 64
LEFT_CHUNKS = 8
BAND_PAST = LEFT_CHUNKS * CHUNK
BAND = BAND_PAST + CHUNK
N_HEADS = 16
HEAD_DIM = D_MODEL // N_HEADS
REL_CLIP = 128
N_REL = 2 * REL_CLIP + 1
CONV_WIDTH = 31
CONV_STATE = CONV_WIDTH - 1
N_GROUPS = 4
EXPERTS_PER_GROUP = 8
N_EXPERTS = N_GROUPS * EXPERTS_PER_GROUP
TOP_K_IN_GROUP = 2
D_EXPERT = D_MODEL // 4
N_MIXERS = 2
N_ATTN_LAYERS = (DEPTH + 1) // 2
N_CONV_LAYERS = DEPTH // 2
RMS_EPS = 1e-6
LN_EPS = 1e-5
KV_KEEP = min(BAND_PAST, PAST_LEN)

kernel_name = 'streaming_chunkattn_conformerconv_hmoe'

def rms_norm(x, g):
    xf = x.astype(jnp.float32)
    y = xf * lax.rsqrt(jnp.mean(xf * xf, axis=-1, keepdims=True) + RMS_EPS)
    return (y * g.astype(jnp.float32)).astype(x.dtype)

def layer_norm(x, g, b):
    xf = x.astype(jnp.float32)
    mu = jnp.mean(xf, axis=-1, keepdims=True)
    xc = xf - mu
    y = xc * lax.rsqrt(jnp.mean(xc * xc, axis=-1, keepdims=True) + LN_EPS)
    return (y * g.astype(jnp.float32) + b.astype(jnp.float32)).astype(x.dtype)

def last_rows(x, n):
    t = x.shape[1]
    if t < n:
        x = jnp.pad(x, ((0, 0), (n - t, 0)) + ((0, 0),) * (x.ndim - 2))
    return x[:, x.shape[1] - n:]

def rel_bias(rel_table, q_pos, k_pos):
    d = jnp.clip(q_pos[:, None] - k_pos[None, :], -REL_CLIP, REL_CLIP) + REL_CLIP
    return rel_table.astype(jnp.float32)[:, d]

def qkv_proj(xn, w_qkv):
    b, t, _ = xn.shape
    qkv = (xn @ w_qkv).reshape(b, t, 3, N_HEADS, HEAD_DIM)
    return qkv[:, :, 0], qkv[:, :, 1], qkv[:, :, 2]

def band_attention_prompt(q, k, v, rel_table):
    b, t, h, dh = q.shape
    n_chunks = t // CHUNK
    pad = ((0, 0), (BAND_PAST, 0), (0, 0), (0, 0))
    k_pad = jnp.pad(k, pad)
    v_pad = jnp.pad(v, pad)
    q_c = q.reshape(b, n_chunks, CHUNK, h, dh).transpose(1, 0, 2, 3, 4)
    bias = rel_bias(rel_table, jnp.arange(CHUNK), jnp.arange(BAND) - BAND_PAST)
    scale = HEAD_DIM ** -0.5
    neg = jnp.finfo(jnp.float32).min

    def one_chunk(args):
        c, qc = args
        start = c * CHUNK
        kb = lax.dynamic_slice_in_dim(k_pad, start, BAND, axis=1)
        vb = lax.dynamic_slice_in_dim(v_pad, start, BAND, axis=1)
        s = jnp.einsum('bqhd,bkhd->bhqk', qc, kb).astype(jnp.float32) * scale + bias
        valid = (start - BAND_PAST + jnp.arange(BAND)) >= 0
        s = jnp.where(valid[None, None, None, :], s, neg)
        p = jax.nn.softmax(s, axis=-1).astype(vb.dtype)
        return jnp.einsum('bhqk,bkhd->bqhd', p, vb)

    out = lax.map(one_chunk, (jnp.arange(n_chunks), q_c))
    return out.transpose(1, 0, 2, 3, 4).reshape(b, t, h * dh)

def band_attention_sample(q, k_all, v_all, rel_table):
    b, tn, h, dh = q.shape
    q_pos = PAST_LEN + jnp.arange(tn)
    k_pos = PAST_LEN - KV_KEEP + jnp.arange(KV_KEEP + tn)
    bias = rel_bias(rel_table, q_pos, k_pos)
    s = jnp.einsum('bqhd,bkhd->bhqk', q, k_all).astype(jnp.float32) * (HEAD_DIM ** -0.5) + bias
    p = jax.nn.softmax(s, axis=-1).astype(v_all.dtype)
    return jnp.einsum('bhqk,bkhd->bqhd', p, v_all).reshape(b, tn, h * dh)

def conv_module(xn, conv_state, w_pw1, b_pw1, w_dw, b_dw, ln_g, ln_b, w_pw2, b_pw2):
    hid = xn @ w_pw1 + b_pw1
    a, g = jnp.split(hid, 2, axis=-1)
    u = a * jax.nn.sigmoid(g)
    u_ext = jnp.concatenate([conv_state.astype(u.dtype), u], axis=1)
    dw = lax.conv_general_dilated(
        u_ext, w_dw[:, None, :].astype(u.dtype), window_strides=(1,), padding='VALID',
        dimension_numbers=('NWC', 'WIO', 'NWC'), feature_group_count=D_MODEL) + b_dw
    z = jax.nn.silu(layer_norm(dw, ln_g, ln_b))
    return z @ w_pw2 + b_pw2, last_rows(u_ext, CONV_STATE)

def hier_moe(xn, w_group, b_group, w_router, b_router, w_gate, w_up, w_down):
    b, t, d = xn.shape
    xt = xn.reshape(b * t, d)
    g_probs = jax.nn.softmax((xt @ w_group).astype(jnp.float32) + b_group.astype(jnp.float32), axis=-1)
    g_w, g_idx = lax.top_k(g_probs, 1)
    e_logits = ((xt @ w_router).astype(jnp.float32) + b_router.astype(jnp.float32)).reshape(
        b * t, N_GROUPS, EXPERTS_PER_GROUP)
    in_group = jnp.take_along_axis(e_logits, g_idx[:, :, None], axis=1)[:, 0]
    top_v, top_i = lax.top_k(in_group, TOP_K_IN_GROUP)
    w2 = jax.nn.softmax(top_v, axis=-1)
    e_idx = g_idx * EXPERTS_PER_GROUP + top_i
    gates = jnp.einsum('nk,nke->ne', g_w * w2, jax.nn.one_hot(e_idx, N_EXPERTS, dtype=jnp.float32))
    y = jnp.zeros_like(xt)
    for grp in range(N_GROUPS):
        sl = slice(grp * EXPERTS_PER_GROUP, (grp + 1) * EXPERTS_PER_GROUP)
        hid = jax.nn.silu(jnp.einsum('nd,edf->nef', xt, w_gate[sl])) * jnp.einsum('nd,edf->nef', xt, w_up[sl])
        hid = hid * gates[:, sl, None].astype(hid.dtype)
        y = y + jnp.einsum('nef,efd->nd', hid, w_down[sl])
    return y.reshape(b, t, d)

def setup_inputs(seed: int = 0) -> dict:
    key = jax.random.key(seed)
    ks = jax.random.split(key, 26)
    f32 = jnp.float32
    D = D_MODEL
    A, C, L = N_ATTN_LAYERS, N_CONV_LAYERS, DEPTH

    def nrm(k, shape, scale):
        return jax.random.normal(k, shape, f32) * scale

    return {
        'x_prompt': nrm(ks[0], (BATCH, SEQ, D), 1.0),
        'x_sample': nrm(ks[1], (DEC_BATCH, DEC_SEQ, D), 1.0),
        'cache_attn_k': nrm(ks[2], (A, DEC_BATCH, KV_KEEP, N_HEADS, HEAD_DIM), 1.0),
        'cache_attn_v': nrm(ks[3], (A, DEC_BATCH, KV_KEEP, N_HEADS, HEAD_DIM), 1.0),
        'cache_conv': nrm(ks[4], (C, DEC_BATCH, CONV_STATE, D), 0.5),
        'norm_mix': 1.0 + nrm(ks[5], (L, D), 0.05),
        'norm_ffn': 1.0 + nrm(ks[6], (L, D), 0.05),
        'norm_final': 1.0 + nrm(ks[7], (D,), 0.05),
        'w_qkv': nrm(ks[8], (A, D, 3 * D), D ** -0.5),
        'w_o': nrm(ks[9], (A, D, D), D ** -0.5),
        'rel_table': nrm(ks[10], (A, N_HEADS, N_REL), 0.5),
        'w_pw1': nrm(ks[11], (C, D, 2 * D), D ** -0.5),
        'b_pw1': nrm(ks[12], (C, 2 * D), 0.02),
        'w_dw': nrm(ks[13], (C, CONV_WIDTH, D), CONV_WIDTH ** -0.5),
        'b_dw': nrm(ks[14], (C, D), 0.02),
        'ln_g': 1.0 + nrm(ks[15], (C, D), 0.05),
        'ln_b': nrm(ks[16], (C, D), 0.02),
        'w_pw2': nrm(ks[17], (C, D, D), D ** -0.5),
        'b_pw2': nrm(ks[18], (C, D), 0.02),
        'w_group': nrm(ks[19], (L, D, N_GROUPS), D ** -0.5),
        'b_group': nrm(ks[20], (L, N_GROUPS), 0.01),
        'w_router': nrm(ks[21], (L, D, N_EXPERTS), D ** -0.5),
        'b_router': nrm(ks[22], (L, N_EXPERTS), 0.01),
        'w_gate': nrm(ks[23], (L, N_EXPERTS, D, D_EXPERT), D ** -0.5),
        'w_up': nrm(ks[24], (L, N_EXPERTS, D, D_EXPERT), D ** -0.5),
        'w_down': nrm(ks[25], (L, N_EXPERTS, D_EXPERT, D), D_EXPERT ** -0.5),
    }

def reference(x_prompt, x_sample, cache_attn_k, cache_attn_v, cache_conv,
              norm_mix, norm_ffn, norm_final,
              w_qkv, w_o, rel_table,
              w_pw1, b_pw1, w_dw, b_dw, ln_g, ln_b, w_pw2, b_pw2,
              w_group, b_group, w_router, b_router, w_gate, w_up, w_down):
    xp, xs = x_prompt, x_sample
    kp_list, vp_list, cp_list = [], [], []
    ks_list, vs_list, cs_list = [], [], []
    for layer in range(DEPTH):
        hp = rms_norm(xp, norm_mix[layer])
        hs = rms_norm(xs, norm_mix[layer])
        if layer % N_MIXERS == 0:
            a = layer // N_MIXERS
            qp, kp, vp = qkv_proj(hp, w_qkv[a])
            op = band_attention_prompt(qp, kp, vp, rel_table[a])
            qs, kn, vn = qkv_proj(hs, w_qkv[a])
            k_all = jnp.concatenate([cache_attn_k[a].astype(kn.dtype), kn], axis=1)
            v_all = jnp.concatenate([cache_attn_v[a].astype(vn.dtype), vn], axis=1)
            os_ = band_attention_sample(qs, k_all, v_all, rel_table[a])
            xp = xp + op @ w_o[a]
            xs = xs + os_ @ w_o[a]
            kp_list.append(last_rows(kp, KV_KEEP))
            vp_list.append(last_rows(vp, KV_KEEP))
            ks_list.append(last_rows(k_all, KV_KEEP))
            vs_list.append(last_rows(v_all, KV_KEEP))
        else:
            c = layer // N_MIXERS
            zero_state = jnp.zeros((hp.shape[0], CONV_STATE, D_MODEL), hp.dtype)
            op, cp = conv_module(hp, zero_state, w_pw1[c], b_pw1[c], w_dw[c], b_dw[c],
                                 ln_g[c], ln_b[c], w_pw2[c], b_pw2[c])
            os_, cs = conv_module(hs, cache_conv[c], w_pw1[c], b_pw1[c], w_dw[c], b_dw[c],
                                  ln_g[c], ln_b[c], w_pw2[c], b_pw2[c])
            xp = xp + op
            xs = xs + os_
            cp_list.append(cp)
            cs_list.append(cs)
        xp = xp + hier_moe(rms_norm(xp, norm_ffn[layer]), w_group[layer], b_group[layer],
                           w_router[layer], b_router[layer], w_gate[layer], w_up[layer], w_down[layer])
        xs = xs + hier_moe(rms_norm(xs, norm_ffn[layer]), w_group[layer], b_group[layer],
                           w_router[layer], b_router[layer], w_gate[layer], w_up[layer], w_down[layer])
    y_prompt = rms_norm(xp, norm_final)
    y_sample = rms_norm(xs, norm_final)
    new_attn_k_prompt = jnp.stack(kp_list)
    new_attn_v_prompt = jnp.stack(vp_list)
    new_conv_prompt = jnp.stack(cp_list)
    new_attn_k_sample = jnp.stack(ks_list)
    new_attn_v_sample = jnp.stack(vs_list)
    new_conv_sample = jnp.stack(cs_list)
    return (y_prompt, y_sample, new_attn_k_prompt, new_attn_v_prompt, new_conv_prompt,
            new_attn_k_sample, new_attn_v_sample, new_conv_sample)


_drawn_inputs = setup_inputs


def setup_inputs(seed=0):
    import zlib

    import numpy as np

    out = dict(_drawn_inputs(seed))
    spreads = {}
    factors = {'ln_b': 2.939}
    for name, (base, spread) in spreads.items():
        noise = np.random.default_rng([zlib.crc32(name.encode()), seed]).standard_normal(out[name].shape)
        drawn = base * np.exp(spread * noise) if base else spread * noise
        out[name] = __import__('jax').numpy.asarray(drawn.astype(out[name].dtype))
    for name, factor in factors.items():
        out[name] = (out[name] * factor).astype(out[name].dtype)
    return out
```

```python
from contextlib import ExitStack

import concourse.bass as bass
from concourse import mybir

F32 = mybir.dt.float32
I32 = mybir.dt.int32
ALU = mybir.AluOpType
ACT = mybir.ActivationFunctionType
AX = mybir.AxisListType

P = 128
TAPS_HALF = 64
BIG = 3.0e38


class Steps:

    def __init__(self, engine, sem):
        self.engine, self.sem, self.base, self.count = engine, sem, 0, 0

    def done(self, instruction):
        instruction.then_inc(self.sem, 1)
        self.count += 1
        self.engine.wait_ge(self.sem, self.base + self.count)

    def enter(self, turn, per_turn):
        self.base, self.start = turn * per_turn + self.count, self.count
        self.count = 0

    def leave(self, turns, per_turn):
        assert self.count == per_turn, self.count
        self.base, self.count = 0, self.start + turns * per_turn


def encoder(nc, x_prompt, x_sample, cache_attn_k, cache_attn_v, cache_conv,
            norm_mix, norm_ffn, norm_final, w_qkv, w_o, rel_rev,
            w_pw1, b_pw1, w_dw, b_dw, ln_g, ln_b, w_pw2, b_pw2,
            w_group, b_group, w_router, b_router, w_gate, w_up, w_down,
            y_prompt, y_sample, kp_out, vp_out, cp_out, ks_out, vs_out, cs_out):
    SEQ, D = x_prompt.shape[1:]
    DEC = x_sample.shape[1]
    TOKENS = SEQ + DEC
    TILES = SEQ // P + 1
    rows = [P] * (TILES - 1) + [DEC]
    C = D // P
    KEEP, HEADS, HD = cache_attn_k.shape[2:]
    PAIRS = HEADS // 2
    NREL = rel_rev.shape[2]
    CHUNK = TAPS_HALF
    TAPS = w_dw.shape[1]
    STATE = TAPS - 1
    GROUPS = w_group.shape[2]
    EXPERTS = w_router.shape[2]
    PER_GROUP = EXPERTS // GROUPS
    FE = w_gate.shape[3]
    FC = FE // P
    LAYERS = w_gate.shape[0]
    HALF = D // 2
    CAP = P // 2
    EPAIRS = EXPERTS // 2
    MAXQ = (TOKENS - 1) // CAP
    OVER = 2 * ((2 * TOKENS // CAP + 1) // 2)
    OPAIRS = OVER // 2
    RC = GROUPS + EXPERTS
    assert HD == CHUNK == DEC and HEADS * HD == D and KEEP == P and C == 8 and FC == 2
    SCALE = float(HD) ** -0.5
    KCOLS = SEQ + KEEP + DEC
    WIN = 2 * P
    EXT = P - 1 + WIN
    SPAN = STATE + SEQ + STATE + DEC
    OUTS = SPAN - STATE
    UNITS = 2 * TILES

    with ExitStack() as ctx:
        def sb(name, shape, dt=F32):
            return ctx.enter_context(nc.sbuf_tensor(name, shape, dt))

        def sem(name):
            return ctx.enter_context(nc.semaphore(name))

        bank = [ctx.enter_context(nc.psum_tensor(f"bank{i}", [P, 512], F32)) for i in range(8)]

        bias_rows = nc.dram_tensor("bias_rows", [P, HEADS, EXT], F32).ap()
        SLOTS = (EXPERTS + OVER) * CAP
        x_sorted = nc.dram_tensor("x_sorted", [SLOTS, D], F32).ap()
        y_sorted = nc.dram_tensor("y_sorted", [SLOTS, D], F32).ap()

        x = sb("x", [P, TILES, D])
        xn_flat = sb("xn_flat", [P, TILES * D])
        xt_flat = sb("xt_flat", [P, TILES * D])
        ring = sb("ring", [P, 2, 2 * 3 * C * FE])
        work = sb("work", [P, 5952])
        gain = sb("gain", [P, 2, D])
        ident = sb("ident", [P, P])
        ones = sb("ones", [P, P])
        lower = sb("lower", [P, P])
        mean_w = sb("mean_w", [P, P])
        router_w = sb("router_w", [P, C, RC])
        router_b = sb("router_b", [P, RC])
        logits = sb("logits", [P, TILES, RC])
        ss = sb("ss", [P, 3, TILES])
        gsc = sb("gsc", [P, 6, TILES, GROUPS])
        esc = sb("esc", [P, 4, TILES, EXPERTS])
        hot = sb("hot", [P, 2, TILES, EXPERTS])
        picked = sb("picked", [P, TILES, EXPERTS])
        tok = sb("tok", [P, 24, TILES])
        down_iota = sb("down_iota", [P, EXPERTS])
        up_iota = sb("up_iota", [P, EXPERTS])
        qrow = sb("qrow", [P, MAXQ])
        qcmp = sb("qcmp", [P, TILES, EXPERTS])
        ecnt = sb("ecnt", [P, 6, EXPERTS])
        orow = sb("orow", [P, OVER])
        ocmp = sb("ocmp", [P, OVER, EXPERTS])
        oexp = sb("oexp", [P, OVER])
        ofew = sb("ofew", [P, OPAIRS])
        opairs = sb("opairs", [P, 1])
        over_expert = sb("over_expert", [P, OVER], I32)
        over_count = sb("over_count", [P, 1], I32)
        down_i = sb("down_i", [P, EXPERTS], I32)
        up_i = sb("up_i", [P, OVER + EXPERTS], I32)
        slot = sb("slot", [P, 2, TILES], I32)
        gate_w = sb("gate_w", [P, 2, TILES])
        soft = sb("soft", [P, 3, 5])

        xn = xn_flat[:].rearrange("p (j d) -> p j d", j=TILES)
        xn_cp = xn_flat[:].rearrange("p (j c q) -> p j q c", j=TILES, c=C)
        xt = xt_flat[:, 0:C * TOKENS].rearrange("p (c t) -> p c t", c=C)
        yg = xt_flat[:].rearrange("p (j d) -> p j d", j=TILES)

        def cut(flat, sizes):
            out, at = [], 0
            for n in sizes:
                out.append(flat[:, at:at + n])
                at += n
            assert at <= flat.shape[1], (at, flat.shape)
            return out

        W3 = 3 * C * P
        part = cut(ring[:, 0, :], [W3, W3] + [2 * TOKENS, KCOLS, (TILES + 1) * P] * 2)
        wa = [part[s].rearrange("p (w c n) -> p w c n", w=3, c=C) for s in range(2)]
        qz = [part[2 + 3 * s].rearrange("p (h t) -> p h t", h=2) for s in range(2)]
        kt = [part[3 + 3 * s] for s in range(2)]
        vv = [part[4 + 3 * s].rearrange("p (j n) -> p j n", j=TILES + 1) for s in range(2)]
        part = cut(ring[:, 1, :], [HEADS * WIN, C * D])
        bias_flat = part[0]
        bias = part[0].rearrange("p (h m) -> p h m", h=HEADS)
        wo_sb = part[1].rearrange("p (c n) -> p c n", c=C)
        part = cut(work[:], [5 * SEQ, 2 * SEQ, 2 * 2 * P, 2 * P, EXT + 1])
        prob = part[0].rearrange("p (b k) -> p b k", b=5)
        pt = part[1].rearrange("p (b k) -> p b k", b=2)
        k_rows = part[2].rearrange("p (s w n) -> p s w n", s=2, w=2)
        kcache = part[3].rearrange("p (s n) -> p s n", s=2)
        rel_sb = part[4]
        ot = xn_flat[:, 0:C * TOKENS].rearrange("p (c t) -> p c t", c=C)

        wgu = [ring[:, s, 0:4 * C * FE].rearrange("p (w e c f) -> p w e c f", w=2, e=2, c=C) for s in range(2)]
        wdn = [ring[:, s, 4 * C * FE:6 * C * FE].rearrange("p (e c n) -> p e c n", e=2, c=FC) for s in range(2)]
        part = cut(work[:], [D, D, D, D, FE, FE, FE, D])
        xe = part[0:2]
        xte = [a.rearrange("p (c r) -> p c r", c=C) for a in part[2:4]]
        sg, hid, hts = part[4], part[5], part[6].rearrange("p (c r) -> p c r", c=FC)
        hid_cp = hid.rearrange("p (c q) -> p q c", c=FC)
        ysb = [part[7], gain[:, 1, :]]

        part = cut(work[:], [2 * C * P, 2 * C * P, SPAN, SPAN, TOKENS])
        wp = [part[s].rearrange("p (w c n) -> p w c n", w=2, c=C) for s in range(2)]
        u = part[2:4]
        sig = part[4]
        dw_flat = xn_flat[:, 0:C * TOKENS]
        dw = dw_flat.rearrange("p (c t) -> p c t", c=C)
        w2 = ring[:, 1, 0:C * D].rearrange("p (c n) -> p c n", c=C)
        NV = TAPS + 5
        rest = ring[:, 1, C * D:]
        PE_TAPS = 6
        part = cut(rest, [C * NV, C * STATE, NV, NV, C * 2 * STATE, OUTS, OUTS, PE_TAPS * P, PE_TAPS * P])
        chan_flat, state_flat, last_flat = part[0], part[1], part[4]
        chan = part[0].rearrange("p (c v) -> p c v", c=C)
        state = part[1].rearrange("p (c k) -> p c k", c=C)
        cvec = part[2:4]
        last_u = part[4].rearrange("p (c k) -> p c k", c=C)
        acc = part[5:7]
        diag = [a.rearrange("p (t q) -> p t q", t=PE_TAPS) for a in part[7:9]]
        raw = gain[:, 1, :]
        sq = xt_flat[:, 0:C * TOKENS]

        x_in = sem("x_in"); small_in = sem("small_in"); gain_in = sem("gain_in"); consts = sem("consts")
        ident0 = sem("ident0")
        rel_in = sem("rel_in"); rel_ext = sem("rel_ext"); rel_out = sem("rel_out"); bias_in = sem("bias_in")
        bias_masked = sem("bias_masked"); zeros_in = sem("zeros_in"); wo_in = sem("wo_in")
        squares = sem("squares"); meansq = sem("meansq"); rooted = sem("rooted"); normed = sem("normed")
        turned = sem("turned"); turn_ev_a = sem("turn_ev_a"); turn_ev_d = sem("turn_ev_d")
        dve_steps = sem("dve_steps"); act_steps = sem("act_steps"); pool_steps = sem("pool_steps")
        wa_in = [sem(f"wa_in{s}") for s in range(2)]; vc_in = [sem(f"vc_in{s}") for s in range(2)]
        q_mm = sem("q_mm"); k_mm = sem("k_mm"); small_mm = sem("small_mm"); v_mm = sem("v_mm"); v4_mm = sem("v4_mm")
        q_ev = sem("q_ev"); k_ev = sem("k_ev"); small_ev = sem("small_ev"); v_ev = sem("v_ev"); v4_ev = sem("v4_ev")
        score_mm = sem("score_mm"); score_free = sem("score_free"); maxed = sem("maxed"); exped = sem("exped")
        probs = sem("probs"); pt_mm = sem("pt_mm"); pt_ev = sem("pt_ev"); os_mm = sem("os_mm"); os_ev = sem("os_ev")
        op_mm = sem("op_mm"); op_ev = sem("op_ev"); krow_mm = sem("krow_mm"); krow_ev = sem("krow_ev")
        kv_out = [sem(f"kv_out{s}") for s in range(2)]
        proj_mm = sem("proj_mm"); proj_ev = sem("proj_ev")
        route_mm = sem("route_mm"); gates_max = sem("gates_max"); gates_exp = sem("gates_exp")
        second = sem("second"); second_exp = sem("second_exp"); picks = sem("picks"); ranks = sem("ranks")
        routed = sem("routed"); scattered = sem("scattered"); gathered = [sem(f"gathered{j}") for j in range(TILES)]
        combined = sem("combined")

        class ExpertSems:

            def __init__(self, tag, slots=2):
                two = lambda n: [sem(f"{tag}_{n}{s}") for s in range(slots)]
                self.y_free = sem(f"{tag}_y_free") if slots == 1 else None
                self.x_in, self.gu_in, self.dn_in, self.y_out = two("x_in"), two("gu_in"), two("dn_in"), two("y_out")
                (self.xt_mm, self.xt_ev_a, self.xt_ev_d, self.gu_mm, self.silu, self.hid, self.ht_mm, self.ht_ev,
                 self.dn_mm, self.y_ev_a, self.y_ev_d) = (
                    sem(f"{tag}_{n}") for n in ("xt_mm", "xt_ev_a", "xt_ev_d", "gu_mm", "silu", "hid", "ht_mm", "ht_ev",
                                                "dn_mm", "y_ev_a", "y_ev_d"))

        base = ExpertSems("ex")
        extras = [ExpertSems(f"ov{l}", 1) for l in range(LAYERS)]
        extra_end = sem("extra_end")
        raw_in = sem("raw_in"); raw_mm = sem("raw_mm"); raw_ev = sem("raw_ev")
        wp_in = [sem(f"wp_in{s}") for s in range(2)]; w2_in = sem("w2_in")
        glu_mm = sem("glu_mm"); sig_done = sem("sig_done"); glu_done = sem("glu_done"); cvec_done = sem("cvec_done")
        u_filled = sem("u_filled"); last_done = sem("last_done"); conv_done = sem("conv_done"); diag_done = sem("diag_done"); conv_mm = sem("conv_mm")
        last_mm = sem("last_mm"); last_ev = sem("last_ev")
        mean_mm = sem("mean_mm"); centred = sem("centred"); sq_done = sem("sq_done"); var_mm = sem("var_mm")
        var_ev = sem("var_ev"); std_done = sem("std_done"); scaled = sem("scaled"); swished = sem("swished")
        y_ready = sem("y_ready"); out_done = sem("out_done")

        dyn = bass.ds
        FREE = 1

        def norm_act(act, steps, n):
            for j in range(TILES):
                r = rows[j]
                wait_x(act, n, j)
                junk = xn if n == 0 else yg
                nc.scalar.activation(junk[0:r, j, :], x[0:r, j, :], ACT.Square,
                                     accum_out=ss[0:r, 0, j:j + 1]).then_inc(squares, 1)
            act.wait_ge(meansq, n + 1)
            nc.scalar.activation(ss[:, 1, :], ss[:, 1, :], ACT.Sqrt).then_inc(rooted, 1)

        def norm_dve(dve, steps, n):
            dve.wait_ge(squares, TILES * (n + 1))
            nc.vector.tensor_scalar(ss[:, 1, :], ss[:, 0, :], 1.0 / D, 1e-6, ALU.mult, ALU.add).then_inc(meansq, 1)
            dve.wait_ge(rooted, n + 1)
            steps.done(nc.vector.reciprocal(ss[:, 2, :], ss[:, 1, :]))
            dve.wait_ge(gain_in, 16 * GAINS[n])
            final = n == 2 * LAYERS
            for j in range(TILES):
                r = rows[j]
                wait_x(dve, n, j)
                out = xn[0:r, j, :] if final else xn_cp[0:r, j, :, :]
                src = x[0:r, j, :] if final else x[0:r, j, :].rearrange("p (q c) -> p q c", c=C)
                g = gain[0:r, 0, :] if final else gain[0:r, 0, :].rearrange("p (q c) -> p q c", c=C)
                nc.vector.scalar_tensor_tensor(out, src, ss[0:r, 2, j:j + 1], g, ALU.mult, ALU.mult).then_inc(normed, 1)

        def turn_pe(pe, n):
            for j in range(TILES):
                r = rows[j]
                pe.wait_ge(normed, TILES * n + j + 1)
                at = TILES * n + j
                if at >= 2:
                    pe.wait_ge(turn_ev_a, at - 1)
                    pe.wait_ge(turn_ev_d, at - 1)
                for c in range(C):
                    b = bank[2 * (at % 2) + c // 4]
                    mm = nc.tensor.transpose(b[:, (c % 4) * P:(c % 4) * P + r], xn[0:r, j, c * P:(c + 1) * P],
                                             ident[0:r, 0:r])
                mm.then_inc(turned, 1)

        def turn_copy(eng, copy, n, j, half, done):
            r, at = rows[j], TILES * n + j
            eng.wait_ge(turned, at + 1)
            src = bank[2 * (at % 2) + half][:].rearrange("p (c t) -> p c t", c=4)
            copy(xt[:, 4 * half:4 * half + 4, j * P:j * P + r], src[:, :, 0:r]).then_inc(done, 1)

        def turn_act(act, n):
            for j in range(TILES):
                turn_copy(act, nc.scalar.copy, n, j, 0, turn_ev_a)

        def turn_dve(dve, n):
            for j in range(TILES):
                turn_copy(dve, nc.vector.tensor_copy, n, j, 1, turn_ev_d)

        def wait_x(eng, n, j):
            if n == 0:
                eng.wait_ge(x_in, 32)
            elif n % 2:
                eng.wait_ge(proj_ev, 2 * TILES * (n // 2) + 2 * (j + 1))
            else:
                eng.wait_ge(combined, TILES * (n // 2 - 1) + j + 1)

        GAINS = {0: 1, 1: 2, 2: 3, 3: 5, 4: 6}
        B_PW2_LOAD = 4

        def broadcast(row):
            return bass.AP(row.tensor, row.offset, [[0, P], [1, row.shape[-1]]])

        def xt_tile(c, j):
            return xt[:, c, j * P:j * P + rows[j]]

        def project_pe(pe, n, act_t, w):
            for j in range(TILES):
                for h in range(2):
                    at = 2 * TILES * n + 2 * j + h
                    if 2 * j + h >= 2:
                        pe.wait_ge(proj_ev, at - 1)
                    b = bank[3 + h]
                    for c in range(C):
                        mm = nc.tensor.matmul(b[0:rows[j], :], act_t[:, c, j * P:j * P + rows[j]],
                                              w[:, c, h * HALF:(h + 1) * HALF], start=c == 0, stop=c == C - 1)
                    mm.then_inc(proj_mm, 1)

        def project_dve(dve, steps, n, bias_row):
            for j in range(TILES):
                for h in range(2):
                    at = 2 * TILES * n + 2 * j + h
                    r, cols = rows[j], slice(h * HALF, (h + 1) * HALF)
                    if bias_row is not None:
                        steps.done(nc.vector.tensor_tensor(x[0:r, j, cols], x[0:r, j, cols], bias_row[0:r, cols], ALU.add))
                    dve.wait_ge(proj_mm, at + 1)
                    nc.vector.tensor_tensor(x[0:r, j, cols], x[0:r, j, cols], bank[3 + h][0:r, :],
                                            ALU.add).then_inc(proj_ev, 1)

        def unit(uu):
            h, i = uu % 2, uu // 2 - 1
            if i < 0:
                return h, None, DEC, KEEP + DEC
            return h, i, P, (i + 1) * P

        PT_LEAD = 5
        SC_LEAD = 2

        def attn_pe(pe):
            def project(n, s, k, step):
                if step == 0:
                    pe.wait_ge(wa_in[s], 64 * (k + 1))
                    pe.wait_ge(v_ev, n)
                    for c in range(C):
                        mm = nc.tensor.matmul(bank[0][:], wa[s][:, 0, c, :], xt[:, c, 0:SEQ], start=c == 0, stop=c == C - 1)
                    mm.then_inc(q_mm, 1)
                if step == 1:
                    pe.wait_ge(v4_ev, n)
                    for c in range(C):
                        mm = nc.tensor.matmul(bank[1][:], wa[s][:, 1, c, :], xt[:, c, 0:SEQ], start=c == 0, stop=c == C - 1)
                    mm.then_inc(k_mm, 1)
                if step == 2:
                    pe.wait_ge(os_ev, n)
                    pe.wait_ge(krow_ev, n)
                    for w in range(2):
                        for c in range(C):
                            nc.tensor.matmul(bank[2][:, w * DEC:(w + 1) * DEC], wa[s][:, w, c, :], xt[:, c, SEQ:TOKENS],
                                             start=c == 0, stop=c == C - 1)
                    nc.tensor.transpose(bank[2][:, P:2 * P], kcache[:, s, :], ident[:, :]).then_inc(small_mm, 1)
                if step == 3:
                    pe.wait_ge(q_ev, n + 1)
                    for j in range(TILES - 1):
                        for c in range(C):
                            mm = nc.tensor.matmul(bank[0][:, j * P:(j + 1) * P], xt_tile(c, j), wa[s][:, 2, c, :],
                                                  start=c == 0, stop=c == C - 1)
                    mm.then_inc(v_mm, 1)
                if step == 4:
                    pe.wait_ge(k_ev, n + 1)
                    for c in range(C):
                        mm = nc.tensor.matmul(bank[1][0:DEC, 0:P], xt_tile(c, TILES - 1), wa[s][:, 2, c, :],
                                              start=c == 0, stop=c == C - 1)
                    mm.then_inc(v4_mm, 1)

            def scores(n, s, uu):
                h, i, q, nk = unit(uu)
                g = n * UNITS + uu
                if uu == 0:
                    pe.wait_ge(q_ev, n + 1)
                    pe.wait_ge(k_ev, n + 1)
                    pe.wait_ge(small_ev, n + 1)
                pe.wait_ge(score_free, g - 1 + SC_LEAD)
                q0 = SEQ if i is None else i * P
                k0 = SEQ if i is None else 0
                nc.tensor.matmul(bank[3 + uu % 2][0:q, 0:nk], qz[s][:, h, q0:q0 + q], kt[s][:, k0:k0 + nk],
                                 start=True, stop=True).then_inc(score_mm, 1)

            def turn(n, s, uu):
                h, i, q, nk = unit(uu)
                g = n * UNITS + uu
                pe.wait_ge(probs, g + 1)
                pe.wait_ge(pt_ev, g - 1 + PT_LEAD)
                b = bank[5 + uu % 2]
                for j in range((nk + P - 1) // P):
                    m = min(P, nk - j * P)
                    if i is None and j == 0:
                        nc.tensor.matmul(b[0:m, 0:q], prob[0:q, uu % 5, 0:m], ident[0:q, 0:q], start=True, stop=True)
                        continue
                    mm = nc.tensor.transpose(b[0:m, j * q:(j + 1) * q], prob[0:q, uu % 5, j * P:j * P + m], ident[0:q, 0:q])
                mm.then_inc(pt_mm, 1)

            def values(n, s, k, uu):
                h, i, q, nk = unit(uu)
                g = n * UNITS + uu
                pe.wait_ge(pt_ev, g + 1 + PT_LEAD)
                if uu == 0:
                    pe.wait_ge(v_ev, n + 1)
                    pe.wait_ge(v4_ev, n + 1)
                    pe.wait_ge(vc_in[s], 16 * (k + 1))
                hd = slice(h * HD, (h + 1) * HD)
                if i is None:
                    nc.tensor.matmul(bank[2][hd, 0:DEC], vv[s][:, TILES, hd], pt[:, uu % 2, 0:DEC], start=True, stop=False)
                    mm = nc.tensor.matmul(bank[2][hd, 0:DEC], vv[s][0:DEC, TILES - 1, hd], pt[0:DEC, uu % 2, DEC:2 * DEC],
                                          start=False, stop=True)
                    if uu == 1:
                        mm.then_inc(os_mm, 1)
                    return
                if uu == 2:
                    pe.wait_ge(op_ev, n + FREE)
                for j in range(i + 1):
                    mm = nc.tensor.matmul(bank[7][hd, i * P:(i + 1) * P], vv[s][:, j, hd], pt[:, uu % 2, j * P:(j + 1) * P],
                                          start=j == 0, stop=j == i)
                if uu == UNITS - 1:
                    mm.then_inc(op_mm, 1)

            def key_rows(n, s):
                pe.wait_ge(os_ev, n + 1)
                nc.tensor.transpose(bank[2][:, 0:P], kt[s][:, SEQ - KEEP:SEQ], ident[:, :])
                nc.tensor.transpose(bank[2][0:DEC, P:2 * P], kt[s][:, SEQ + KEEP:KCOLS], ident[:, :]).then_inc(krow_mm, 1)

            def pair(n, s, k, more):
                s2, k2 = (s + 1) % 2, k + (s + 1) // 2
                scores(n, s, 0)
                scores(n, s, 1)
                if more:
                    project(n + 1, s2, k2, 0)
                for uu in range(UNITS):
                    if uu + 2 < UNITS:
                        scores(n, s, uu + 2)
                    turn(n, s, uu)
                    if uu >= 1:
                        values(n, s, k, uu - 1)
                    if uu == 2 and more:
                        project(n + 1, s2, k2, 1)
                    if uu == 4:
                        key_rows(n, s)
                    if uu == 6 and more:
                        project(n + 1, s2, k2, 2)
                    if uu == 7 and more:
                        project(n + 1, s2, k2, 3)
                    if uu == 9 and more:
                        project(n + 1, s2, k2, 4)
                values(n, s, k, UNITS - 1)

            pe.wait_ge(turn_ev_a, TILES)
            pe.wait_ge(turn_ev_d, TILES)
            pe.wait_ge(consts, CONSTS)
            for step in range(5):
                project(0, 0, 0, step)
            with pe.Fori(0, PAIRS // 2 - 1) as it:
                for s in range(2):
                    pair(2 * it + s, s, it, True)
            for s in range(2):
                pair(PAIRS - 2 + s, s, PAIRS // 2 - 1, s == 0)

        def attn_act(act, steps):
            def query_copy(n, s):
                act.wait_ge(q_mm, n + 1)
                for h in range(2):
                    hd = slice(h * HD, (h + 1) * HD)
                    ins = nc.scalar.activation(qz[s][hd, h, 0:SEQ], bank[0][hd, :], ACT.Copy, scale=SCALE)
                ins.then_inc(q_ev, 1)

            def small_copy(n, s):
                act.wait_ge(small_mm, n + 1)
                for h in range(2):
                    hd = slice(h * HD, (h + 1) * HD)
                    nc.scalar.activation(qz[s][hd, h, SEQ:TOKENS], bank[2][hd, 0:DEC], ACT.Copy, scale=SCALE)
                nc.scalar.copy(kt[s][:, SEQ + KEEP:KCOLS], bank[2][:, DEC:2 * DEC])
                nc.scalar.copy(kt[s][:, SEQ:SEQ + KEEP], bank[2][:, P:2 * P]).then_inc(small_ev, 1)

            def key_row_copy(n, s, k):
                act.wait_ge(krow_mm, n + 1)
                act.wait_ge(kv_out[s], 64 * k + 16)
                nc.scalar.copy(k_rows[:, s, 0, :], bank[2][:, 0:P])
                nc.scalar.copy(k_rows[0:DEC, s, 1, :], bank[2][0:DEC, P:2 * P]).then_inc(krow_ev, 1)

            def exps(n, uu):
                h, i, q, nk = unit(uu)
                act.wait_ge(maxed, n * UNITS + uu + 1)
                b = uu % 5
                nc.scalar.activation(prob[0:q, b, 0:nk], prob[0:q, b, 0:nk], ACT.Exp, bias=soft[0:q, 0, b:b + 1],
                                     accum_out=soft[0:q, 1, b:b + 1]).then_inc(exped, 1)

            def pt_copy(n, uu):
                h, i, q, nk = unit(uu)
                act.wait_ge(pt_mm, n * UNITS + uu + 1)
                b = uu % 2
                if i is None:
                    nc.scalar.copy(pt[:, b, 0:DEC], bank[5 + b][:, 0:DEC])
                    nc.scalar.copy(pt[0:DEC, b, DEC:2 * DEC], bank[5 + b][0:DEC, DEC:2 * DEC]).then_inc(pt_ev, 1)
                else:
                    nc.scalar.copy(pt[:, b, 0:nk], bank[5 + b][:, 0:nk]).then_inc(pt_ev, 1)

            def pair(n, s, k, more):
                s2 = (s + 1) % 2
                exps(n, 0)
                exps(n, 1)
                if more:
                    query_copy(n + 1, s2)
                for uu in range(UNITS):
                    pt_copy(n, uu)
                    if uu + 2 < UNITS:
                        exps(n, uu + 2)
                    if uu == 5:
                        key_row_copy(n, s, k)
                    if uu == 7 and more:
                        small_copy(n + 1, s2)

            act.sem_inc(pt_ev, PT_LEAD)
            act.sem_inc(last_done, FREE)
            for m in (base, *extras):
                act.sem_inc(m.xt_ev_a, FREE)
                act.sem_inc(m.y_ev_a, FREE)
            act.wait_ge(consts, CONSTS)
            query_copy(0, 0)
            small_copy(0, 0)
            with act.Fori(0, PAIRS // 2 - 1) as it:
                for s in range(2):
                    pair(2 * it + s, s, it, True)
            for s in range(2):
                pair(PAIRS - 2 + s, s, PAIRS // 2 - 1, s == 0)

        def attn_dve(dve, steps):
            def key_copy(n, s):
                dve.wait_ge(k_mm, n + 1)
                nc.vector.tensor_copy(kt[s][:, 0:SEQ], bank[1][:]).then_inc(k_ev, 1)

            def value_copy(n, s, k):
                dve.wait_ge(v_mm, n + 1)
                dve.wait_ge(kv_out[s], 64 * k + 16)
                nc.vector.tensor_copy(vv[s][:, 0:TILES - 1, :], bank[0][:].rearrange("p (j n) -> p j n", n=P)).then_inc(v_ev, 1)

            def value4_copy(n, s, k):
                dve.wait_ge(v4_mm, n + 1)
                dve.wait_ge(kv_out[s], 64 * k + 16)
                nc.vector.tensor_copy(vv[s][0:DEC, TILES - 1, :], bank[1][0:DEC, 0:P]).then_inc(v4_ev, 1)

            def add_bias(n, uu):
                h, i, q, nk = unit(uu)
                g = n * UNITS + uu
                b, src = uu % 5, bank[3 + uu % 2]
                dve.wait_ge(score_mm, g + 1)
                dve.wait_ge(pt_ev, g - 4 + PT_LEAD)
                hh = 2 * n + h
                if i is None:
                    near, b0, far = nk, 0, 0
                else:
                    near = min(nk, WIN)
                    b0, far = WIN - near, nk - near
                if far:
                    nc.vector.tensor_scalar(prob[0:q, b, 0:far], src[0:q, 0:far], bias_flat[0:q, dyn(hh * WIN, 1)], None, ALU.add)
                nc.vector.tensor_tensor(prob[0:q, b, far:nk], src[0:q, far:nk],
                                        bias_flat[0:q, dyn(hh * WIN + b0, near)], ALU.add).then_inc(score_free, 1)
                dve.wait_ge(score_free, g + 1 + SC_LEAD)
                nc.vector.tensor_reduce(soft[0:q, 0, b:b + 1], prob[0:q, b, 0:nk], AX.X, ALU.max,
                                        negate=True).then_inc(maxed, 1)

            def normalise(n, uu):
                h, i, q, nk = unit(uu)
                b = uu % 5
                dve.wait_ge(exped, n * UNITS + uu + 1)
                steps.done(nc.vector.reciprocal(soft[0:q, 2, b:b + 1], soft[0:q, 1, b:b + 1]))
                nc.vector.tensor_scalar(prob[0:q, b, 0:nk], prob[0:q, b, 0:nk], soft[0:q, 2, b:b + 1], None,
                                        ALU.mult).then_inc(probs, 1)

            def sample_copy(n):
                dve.wait_ge(os_mm, n + 1)
                nc.vector.tensor_copy(xn_flat[:, dyn(n * TOKENS + SEQ, DEC)], bank[2][:, 0:DEC]).then_inc(os_ev, 1)

            def prompt_copy(n):
                dve.wait_ge(op_mm, n + 1)
                nc.vector.tensor_copy(xn_flat[:, dyn(n * TOKENS, SEQ)], bank[7][:]).then_inc(op_ev, 1)

            def pair(n, s, k, more):
                s2, k2 = (s + 1) % 2, k + (s + 1) // 2
                add_bias(n, 0)
                add_bias(n, 1)
                for uu in range(UNITS):
                    normalise(n, uu)
                    if uu + 2 < UNITS:
                        add_bias(n, uu + 2)
                    if uu == 3:
                        sample_copy(n)
                        if more:
                            key_copy(n + 1, s2)
                    if uu == 9 and more:
                        value_copy(n + 1, s2, k2)
                        value4_copy(n + 1, s2, k2)
                prompt_copy(n)

            dve.sem_inc(score_free, SC_LEAD)
            for begins_free in (op_ev, *(x for m in (base, *extras) for x in (m.xt_ev_d, m.y_ev_d, m.hid))):
                dve.sem_inc(begins_free, FREE)
            dve.wait_ge(bias_in, 16)
            nc.vector.memset(bias[0:CHUNK, :, WIN - CHUNK:WIN], -BIG).then_inc(bias_masked, 1)
            dve.wait_ge(bias_masked, 1)
            key_copy(0, 0)
            value_copy(0, 0, 0)
            value4_copy(0, 0, 0)
            PER = 2 * UNITS
            with dve.Fori(0, PAIRS // 2 - 1) as it:
                steps.enter(it, PER)
                for s in range(2):
                    pair(2 * it + s, s, it, True)
            steps.leave(PAIRS // 2 - 1, PER)
            for s in range(2):
                pair(PAIRS - 2 + s, s, PAIRS // 2 - 1, s == 0)

        def cols(n):
            return dyn(n * P, P)

        def heads2d(a):
            return a.rearrange("t h d -> t (h d)")

        def attn_sync(sp):
            wq = w_qkv[0].rearrange("(p c) n -> p c n", c=C)

            def load(n, s):
                for w in range(3):
                    sp.dma_start(wa[s][:, w, :, :], wq[:, :, dyn(w * D + n * P, P)]).then_inc(wa_in[s], 16)
                sp.dma_start(kcache[:, s, :], heads2d(cache_attn_k[0, 0])[:, cols(n)]).then_inc(wa_in[s], 16)

            def load_v(n, s):
                sp.dma_start(vv[s][:, TILES, :], heads2d(cache_attn_v[0, 0])[:, cols(n)]).then_inc(vc_in[s], 16)

            sp.dma_start(rel_sb[0:HEADS, P - 1:P - 1 + WIN], rel_rev[0, :, 0:WIN]).then_inc(rel_in, 16)
            load(0, 0)
            load_v(0, 0)
            sp.wait_ge(rel_ext, 1)
            sp.dma_start(bias_rows.rearrange("r h m -> h r m"),
                         rel_sb[0:HEADS, 0:EXT].unsqueeze(1).to_broadcast([HEADS, P, EXT])).then_inc(rel_out, 16)
            load(1, 1)
            load_v(1, 1)
            sp.wait_ge(rel_out, 16)
            sp.dma_start(bias, bass.AP(bias_rows.tensor, P - 1, [[HEADS * EXT - 1, P], [EXT, HEADS], [1, WIN]])).then_inc(bias_in, 16)
            sp.dma_start(wo_sb, w_o[0].rearrange("(c p) n -> p c n", p=P)).then_inc(wo_in, 16)
            with sp.Fori(0, PAIRS // 2 - 1) as it:
                for s in range(2):
                    n = 2 * it + s
                    sp.wait_ge(v4_mm, n + 1)
                    load(n + 2, s)
                    sp.wait_ge(os_mm, n + 1)
                    load_v(n + 2, s)
            sp.wait_ge(consts, CONSTS)
            for s, (a, b) in enumerate(((0, OPAIRS // 2), (OPAIRS // 2, OPAIRS))):
                sp.dma_start(y_sorted[EXPERTS * CAP + a * P:EXPERTS * CAP + b * P, :].rearrange("(a p) d -> p a d", p=P),
                             gain[:, 1, :].unsqueeze(1).to_broadcast([P, b - a, D])).then_inc(base.y_out[s], 16)

        def attn_pool(pool):
            def store(n, s):
                pool.wait_ge(krow_ev, n + 1)
                pool.wait_ge(v_ev, n + 1)
                pool.wait_ge(v4_ev, n + 1)
                for src, dst in ((k_rows[:, s, 0, :], kp_out[0, 0]), (vv[s][:, TILES - 2, :], vp_out[0, 0])):
                    pool.dma_start(heads2d(dst)[:, cols(n)], src).then_inc(kv_out[s], 16)
                for src, dst in ((k_rows[0:DEC, s, 1, :], ks_out[0, 0]), (vv[s][0:DEC, TILES - 1, :], vs_out[0, 0])):
                    pool.dma_start(heads2d(dst)[KEEP - DEC:KEEP, cols(n)], src).then_inc(kv_out[s], 16)

            zeros = lambda a: gain[:, 1, :].unsqueeze(1).to_broadcast([P, a, D])
            x_rows = x_sorted.rearrange("(a p) d -> p a d", p=P)
            few = SLOTS // P // PAIRS
            with pool.Fori(0, PAIRS // 2) as it:
                for s in range(2):
                    store(2 * it + s, s)
                    pool.dma_start(x_rows[:, dyn((2 * it + s) * few, few), :], zeros(few)).then_inc(zeros_in, 16)
            rest = SLOTS // P - PAIRS * few
            pool.dma_start(x_rows[:, PAIRS * few:SLOTS // P, :], zeros(rest)).then_inc(zeros_in, 16)

        def router_pe(pe, l):
            pe.wait_ge(turn_ev_a, TILES * (2 * l + 2))
            pe.wait_ge(turn_ev_d, TILES * (2 * l + 2))
            pe.wait_ge(small_in, 64 * (l + 1))
            for j in range(TILES):
                for c in range(C):
                    mm = nc.tensor.matmul(bank[4][0:rows[j], j * RC:(j + 1) * RC], xt_tile(c, j), router_w[:, c, :],
                                          start=c == 0, stop=c == C - 1)
            mm.then_inc(route_mm, 1)
            pe.wait_ge(picks, l + 1)
            nc.tensor.matmul(bank[5][:, 0:TILES * EXPERTS], lower[:], picked[:].rearrange("p j e -> p (j e)"),
                             start=True, stop=False)
            for back in range(1, TILES):
                nc.tensor.matmul(bank[5][:, back * EXPERTS:TILES * EXPERTS], ones[:],
                                 picked[:, 0:TILES - back, :].rearrange("p j e -> p (j e)"),
                                 start=False, stop=back == TILES - 1)
            for j in range(TILES):
                mm = nc.tensor.matmul(bank[6][:, 0:EXPERTS], ones[:], picked[:, j, :], start=j == 0, stop=j == TILES - 1)
            mm.then_inc(ranks, 1)

        def router_act(act, l):
            act.wait_ge(gates_max, l + 1)
            nc.scalar.activation(gsc[:, 1, :, :], gsc[:, 1, :, :], ACT.Exp).then_inc(gates_exp, 1)
            act.wait_ge(second, l + 1)
            nc.scalar.activation(tok[:, 4, :], tok[:, 4, :], ACT.Exp).then_inc(second_exp, 1)

        def router_dve(dve, steps, l):
            V, do = nc.vector, steps.done

            def wide(a, n):
                return a.unsqueeze(2).to_broadcast([P, TILES, n])

            def over_tiles(a):
                return a.unsqueeze(1).to_broadcast([P, TILES, a.shape[1]])

            def first_of(out, values, top, n, tmp):
                do(V.tensor_tensor(out, values, wide(top, n), ALU.is_equal))
                do(V.tensor_tensor(out, out, over_tiles(down_iota[:, 0:n]), ALU.mult))
                do(V.tensor_reduce(tmp, out, AX.X, ALU.max))
                do(V.tensor_tensor(out, out, wide(tmp, n), ALU.is_equal))

            dve.wait_ge(route_mm, l + 1)
            do(V.tensor_tensor(logits[:, 0:TILES - 1, :], bank[4][:, 0:(TILES - 1) * RC].rearrange("p (j n) -> p j n", n=RC),
                               router_b[:].unsqueeze(1).to_broadcast([P, TILES - 1, RC]), ALU.add))
            do(V.tensor_tensor(logits[0:DEC, TILES - 1, :], bank[4][0:DEC, (TILES - 1) * RC:TILES * RC],
                               router_b[0:DEC, :], ALU.add))
            lg, le = logits[:, :, 0:GROUPS], logits[:, :, GROUPS:RC]
            do(V.tensor_reduce(tok[:, 0, :], lg, AX.X, ALU.max))
            V.tensor_tensor(gsc[:, 1, :, :], lg, wide(tok[:, 0, :], GROUPS), ALU.subtract).then_inc(gates_max, 1)
            first_of(gsc[:, 0, :, :], lg, tok[:, 0, :], GROUPS, tok[:, 1, :])
            do(V.tensor_scalar(gsc[:, 2, :, :], gsc[:, 0, :, :], BIG, -BIG, ALU.mult, ALU.add))
            spread = lambda a: a.unsqueeze(3).to_broadcast([P, TILES, GROUPS, PER_GROUP])
            grouped = lambda a: a.rearrange("p j (g e) -> p j g e", g=GROUPS)
            do(V.tensor_tensor(grouped(esc[:, 0, :, :]), grouped(le), spread(gsc[:, 0, :, :]), ALU.mult))
            do(V.tensor_tensor(grouped(esc[:, 0, :, :]), grouped(esc[:, 0, :, :]), spread(gsc[:, 2, :, :]), ALU.add))
            do(V.tensor_reduce(tok[:, 2, :], esc[:, 0, :, :], AX.X, ALU.max))
            first_of(hot[:, 0, :, :], esc[:, 0, :, :], tok[:, 2, :], EXPERTS, tok[:, 1, :])
            do(V.tensor_scalar(esc[:, 1, :, :], hot[:, 0, :, :], -BIG, None, ALU.mult))
            do(V.tensor_tensor(esc[:, 1, :, :], esc[:, 1, :, :], esc[:, 0, :, :], ALU.add))
            do(V.tensor_reduce(tok[:, 3, :], esc[:, 1, :, :], AX.X, ALU.max))
            V.tensor_tensor(tok[:, 4, :], tok[:, 3, :], tok[:, 2, :], ALU.subtract).then_inc(second, 1)
            first_of(hot[:, 1, :, :], esc[:, 1, :, :], tok[:, 3, :], EXPERTS, tok[:, 1, :])
            do(V.memset(hot[DEC:P, :, TILES - 1, :], 0.0))
            V.tensor_tensor(picked[:], hot[:, 0, :, :], hot[:, 1, :, :], ALU.add).then_inc(picks, 1)
            dve.wait_ge(gates_exp, l + 1)
            do(V.tensor_reduce(tok[:, 5, :], gsc[:, 1, :, :], AX.X, ALU.add))
            dve.wait_ge(second_exp, l + 1)
            do(V.tensor_scalar(tok[:, 6, :], tok[:, 4, :], 1.0, None, ALU.add))
            do(V.tensor_tensor(tok[:, 6, :], tok[:, 6, :], tok[:, 5, :], ALU.mult))
            do(V.reciprocal(gate_w[:, 0, :], tok[:, 6, :]))
            do(V.tensor_tensor(gate_w[:, 1, :], gate_w[:, 0, :], tok[:, 4, :], ALU.mult))
            dve.wait_ge(ranks, l + 1)
            do(V.tensor_copy(ecnt[:, 0, :], bank[6][:, 0:EXPERTS]))
            do(V.memset(ecnt[:, 1, :], 0.0))
            for q in range(MAXQ):
                do(V.tensor_scalar(ecnt[:, 2, :], ecnt[:, 0, :], float(CAP * (q + 1)), None, ALU.is_gt))
                do(V.tensor_tensor(ecnt[:, 1, :], ecnt[:, 1, :], ecnt[:, 2, :], ALU.add))
            do(V.memset(ecnt[:, 3, :], 0.0))
            do(V.tensor_tensor_scan(ecnt[:, 4, :], ecnt[:, 1, :], ecnt[:, 3, :], 0.0, ALU.add, ALU.add))
            do(V.tensor_tensor(ecnt[:, 5, :], ecnt[:, 4, :], ecnt[:, 1, :], ALU.subtract))
            do(V.tensor_tensor(ocmp[:], orow[:].unsqueeze(2).to_broadcast([P, OVER, EXPERTS]),
                               ecnt[:, 4, :].unsqueeze(1).to_broadcast([P, OVER, EXPERTS]), ALU.is_ge))
            do(V.tensor_reduce(oexp[:], ocmp[:], AX.X, ALU.add))
            do(V.tensor_scalar(over_expert[:], oexp[:], float(EXPERTS - 1), None, ALU.min))
            do(V.tensor_scalar(ofew[:], orow[:, 0:OVER:2], ecnt[:, 4, EXPERTS - 1:EXPERTS], None, ALU.is_lt))
            do(V.tensor_reduce(opairs[:], ofew[:], AX.X, ALU.add))
            do(V.tensor_copy(over_count[:], opairs[:]))
            for k in range(2):
                h = hot[:, k, :, :]
                for out, col in ((7, bank[5][:, 0:TILES * EXPERTS].rearrange("p (j e) -> p j e", e=EXPERTS)),
                                 (8, over_tiles(up_iota[:])), (9, over_tiles(ecnt[:, 5, :]))):
                    do(V.tensor_tensor(qcmp[:], h, col, ALU.mult))
                    do(V.tensor_reduce(tok[:, out, :], qcmp[:], AX.X, ALU.add))
                do(V.memset(tok[:, 10, :], 0.0))
                for q in range(MAXQ):
                    do(V.tensor_scalar(tok[:, 11, :], tok[:, 7, :], float(CAP * (q + 1)), None, ALU.is_ge))
                    do(V.tensor_tensor(tok[:, 10, :], tok[:, 10, :], tok[:, 11, :], ALU.add))
                do(V.tensor_tensor(tok[:, 12, :], tok[:, 9, :], tok[:, 8, :], ALU.subtract))
                do(V.tensor_tensor(tok[:, 12, :], tok[:, 12, :], tok[:, 10, :], ALU.add))
                do(V.tensor_scalar(tok[:, 12, :], tok[:, 12, :], float(EXPERTS - 1), None, ALU.add))
                do(V.tensor_scalar(tok[:, 13, :], tok[:, 10, :], 0.0, None, ALU.is_gt))
                do(V.tensor_tensor(tok[:, 12, :], tok[:, 12, :], tok[:, 13, :], ALU.mult))
                do(V.tensor_tensor(tok[:, 12, :], tok[:, 12, :], tok[:, 8, :], ALU.add))
                do(V.tensor_tensor(tok[:, 12, :], tok[:, 12, :], tok[:, 10, :], ALU.subtract))
                do(V.scalar_tensor_tensor(tok[:, 14, :], tok[:, 12, :], float(CAP), tok[:, 7, :], ALU.mult, ALU.add))
                V.tensor_copy(slot[:, k, :], tok[:, 14, :]).then_inc(routed, 1)

        def scatter_pool(pool, l):
            pool.wait_ge(routed, 2 * (l + 1))
            pool.wait_ge(normed, TILES * (2 * l + 2))
            if l == 0:
                pool.wait_ge(zeros_in, 16 * (PAIRS + 1))
            for j in range(TILES):
                for k in range(2):
                    pool.indirect_dma_start(x_sorted, bass.IndirectOffsetOnAxis(slot[0:rows[j], k, j:j + 1], 0),
                                            xn[0:rows[j], j, :], None, bounds_check=SLOTS - 1,
                                            oob_is_err=True).then_inc(scattered, 16)

        def gather_pool(pool, l):
            for s in range(2):
                pool.wait_ge(base.y_out[s], 16 * (EPAIRS // 2) * (l + 1) + 16)
            pool.wait_ge(extra_end, l + 1)
            pool.wait_ge(scattered, 16 * 2 * TILES * (l + 1))
            for j in range(TILES):
                for k in range(2):
                    dst = (xn, yg)[k]
                    pool.indirect_dma_start(dst[0:rows[j], j, :], None, y_sorted,
                                            bass.IndirectOffsetOnAxis(slot[0:rows[j], k, j:j + 1], 0),
                                            bounds_check=SLOTS - 1, oob_is_err=True).then_inc(gathered[j], 16)

        def combine_dve(dve, steps, l):
            for j in range(TILES):
                r = rows[j]
                dve.wait_ge(gathered[j], 32 * (l + 1))
                steps.done(nc.vector.scalar_tensor_tensor(x[0:r, j, :], xn[0:r, j, :], gate_w[0:r, 0, j:j + 1],
                                                          x[0:r, j, :], ALU.mult, ALU.add))
                nc.vector.scalar_tensor_tensor(x[0:r, j, :], yg[0:r, j, :], gate_w[0:r, 1, j:j + 1],
                                               x[0:r, j, :], ALU.mult, ALU.add).then_inc(combined, 1)

        def ex_turn_pe(pe, m, i, s, k):
            pe.wait_ge(m.x_in[s], 16 * (k + 1))
            pe.wait_ge(m.xt_ev_a, i + FREE)
            pe.wait_ge(m.xt_ev_d, i + FREE)
            for c in range(C):
                mm = nc.tensor.transpose(bank[c // 4][:, (c % 4) * P:(c % 4 + 1) * P], xe[s][:, c * P:(c + 1) * P], ident[:])
            mm.then_inc(m.xt_mm, 1)

        def ex_up_pe(pe, m, i, s, k, loads):
            pe.wait_ge(m.xt_ev_a, i + 1 + FREE)
            pe.wait_ge(m.xt_ev_d, i + 1 + FREE)
            pe.wait_ge(m.gu_in[s], 16 * loads * (k + 1))
            for c in range(C):
                for e in range(2):
                    rr = slice(CAP * e, CAP * (e + 1))
                    mm = nc.tensor.matmul(bank[2 + s][rr, :], xte[s][:, c, rr], wgu[s][:, :, e, c, :],
                                          start=c == 0, stop=c == C - 1)
            mm.then_inc(m.gu_mm, 1)

        def ex_down_pe(pe, m, i, s, k, loads):
            pe.wait_ge(m.hid, i + 1 + FREE)
            for c in range(FC):
                mm = nc.tensor.transpose(bank[4][:, c * P:(c + 1) * P], hid[:, c * P:(c + 1) * P], ident[:])
            mm.then_inc(m.ht_mm, 1)
            pe.wait_ge(m.ht_ev, i + 1)
            pe.wait_ge(m.dn_in[s], 16 * loads * (k + 1))
            pe.wait_ge(m.y_ev_a, i + FREE)
            pe.wait_ge(m.y_ev_d, i + FREE)
            for h in range(2):
                for c in range(FC):
                    for e in range(2):
                        rr = slice(CAP * e, CAP * (e + 1))
                        mm = nc.tensor.matmul(bank[5 + h][rr, :], hts[:, c, rr], wdn[s][:, e, c, h * HALF:(h + 1) * HALF],
                                              start=c == 0, stop=c == FC - 1)
            mm.then_inc(m.dn_mm, 1)

        def ex_turn_copy(eng, copy, m, i, s, half, done):
            eng.wait_ge(m.xt_mm, i + 1)
            copy(xte[s][:, 4 * half:4 * half + 4, :], bank[half][:].rearrange("p (c r) -> p c r", c=4)).then_inc(done, 1)

        def ex_silu_act(act, m, i, s):
            act.wait_ge(m.gu_mm, i + 1)
            act.wait_ge(m.hid, i + FREE)
            nc.scalar.activation(sg, bank[2 + s][:, 0:FE], ACT.Silu).then_inc(m.silu, 1)

        def ex_hid_dve(dve, m, i, s):
            dve.wait_ge(m.silu, i + 1)
            nc.vector.tensor_tensor(hid_cp, sg.rearrange("p (q c) -> p q c", c=FC),
                                    bank[2 + s][:, FE:2 * FE].rearrange("p (q c) -> p q c", c=FC), ALU.mult).then_inc(m.hid, 1)

        def ex_ht_dve(dve, m, i):
            dve.wait_ge(m.ht_mm, i + 1)
            nc.vector.tensor_copy(hts, bank[4][:, 0:FE].rearrange("p (c r) -> p c r", c=FC)).then_inc(m.ht_ev, 1)

        def ex_y_copy(eng, copy, m, i, s, k, half, done):
            eng.wait_ge(m.dn_mm, i + 1)
            if m is base:
                eng.wait_ge(m.y_out[s], 16 * k + 16)
            else:
                eng.wait_ge(m.y_free, i + FREE)
            copy(ysb[s][:, half * HALF:(half + 1) * HALF], bank[5 + half][:]).then_inc(done, 1)

        def rows_of(a, i):
            return a[dyn(i * P, P), :]

        def turns(eng, body, l, steps=None):
            first = EPAIRS * l
            with eng.Fori(0, EPAIRS // 2 - 1) as it:
                for s in range(2):
                    body(first + 2 * it + s, s, first // 2 + it, 2 * it + s, True)
            for s in range(2):
                body(first + EPAIRS - 2 + s, s, (first + EPAIRS) // 2 - 1, EPAIRS - 2 + s, s == 0)

        def extra_turns(eng, l, body):
            count = eng.value_load(over_count[0:1, 0:1], min_val=0, max_val=OPAIRS)
            with eng.If(count > 0):
                with eng.Fori(0, count) as it:
                    body(it)

        def experts_pe(pe, l):
            ex_turn_pe(pe, base, EPAIRS * l, 0, EPAIRS // 2 * l)

            def body(i, s, k, local, more):
                ex_up_pe(pe, base, i, s, k, 2)
                if more:
                    ex_turn_pe(pe, base, i + 1, (s + 1) % 2, k + (s + 1) // 2)
                ex_down_pe(pe, base, i, s, k, 1)

            turns(pe, body, l)

            extra = extras[l]

            def further(i):
                ex_turn_pe(pe, extra, i, 0, i)
                ex_up_pe(pe, extra, i, 0, i, 4)
                ex_down_pe(pe, extra, i, 0, i, 2)

            extra_turns(pe, l, further)

        def experts_act(act, l):
            ex_turn_copy(act, nc.scalar.copy, base, EPAIRS * l, 0, 0, base.xt_ev_a)

            def body(i, s, k, local, more):
                ex_silu_act(act, base, i, s)
                if more:
                    ex_turn_copy(act, nc.scalar.copy, base, i + 1, (s + 1) % 2, 0, base.xt_ev_a)
                ex_y_copy(act, nc.scalar.copy, base, i, s, k, 0, base.y_ev_a)

            turns(act, body, l)

            extra = extras[l]

            def further(i):
                ex_turn_copy(act, nc.scalar.copy, extra, i, 0, 0, extra.xt_ev_a)
                ex_silu_act(act, extra, i, 0)
                ex_y_copy(act, nc.scalar.copy, extra, i, 0, i, 0, extra.y_ev_a)

            extra_turns(act, l, further)

        def experts_dve(dve, l):
            ex_turn_copy(dve, nc.vector.tensor_copy, base, EPAIRS * l, 0, 1, base.xt_ev_d)

            def body(i, s, k, local, more):
                ex_hid_dve(dve, base, i, s)
                if more:
                    ex_turn_copy(dve, nc.vector.tensor_copy, base, i + 1, (s + 1) % 2, 1, base.xt_ev_d)
                ex_ht_dve(dve, base, i)
                ex_y_copy(dve, nc.vector.tensor_copy, base, i, s, k, 1, base.y_ev_d)

            turns(dve, body, l)

            extra = extras[l]

            def further(i):
                ex_turn_copy(dve, nc.vector.tensor_copy, extra, i, 0, 1, extra.xt_ev_d)
                ex_hid_dve(dve, extra, i, 0)
                ex_ht_dve(dve, extra, i)
                ex_y_copy(dve, nc.vector.tensor_copy, extra, i, 0, i, 1, extra.y_ev_d)

            extra_turns(dve, l, further)

        def gu_load(sp, l, p, s):
            for w, src in enumerate((w_gate, w_up)):
                sp.dma_start(wgu[s][:, w, :, :, :].rearrange("p e c f -> p e (c f)"),
                             src[l, dyn(2 * p, 2)].rearrange("e (p c) f -> p e (c f)", c=C)).then_inc(base.gu_in[s], 16)

        def dn_load(sp, l, p, s):
            sp.dma_start(wdn[s].rearrange("p e c n -> p e (c n)"),
                         w_down[l, dyn(2 * p, 2)].rearrange("e (p c) n -> p e (c n)", c=FC)).then_inc(base.dn_in[s], 16)

        def first_loads(sp, l, s):
            if s == 0 and l == 0:
                sp.wait_ge(op_ev, PAIRS + FREE)
                for b in range(2):
                    sp.wait_ge(kv_out[b], 64 * PAIRS // 2 + 16)
            if s == 1:
                sp.wait_ge(proj_ev, 2 * TILES * (l + 1))
            gu_load(sp, l, s, s)
            dn_load(sp, l, s, s)

        def experts_sync(sp, l):
            sp.wait_ge(scattered, 16 * 2 * TILES * (l + 1))
            for s in range(2):
                sp.dma_start(xe[s], rows_of(x_sorted, s)).then_inc(base.x_in[s], 16)

            def body(i, s, k, local, more):
                if local is not None and not isinstance(local, int):
                    sp.wait_ge(base.xt_mm, i + 1)
                    sp.dma_start(xe[s], rows_of(x_sorted, local + 2)).then_inc(base.x_in[s], 16)
                    sp.wait_ge(base.gu_mm, i + 1)
                    gu_load(sp, l, local + 2, s)
                    sp.wait_ge(base.dn_mm, i + 1)
                    dn_load(sp, l, local + 2, s)
                sp.wait_ge(base.y_ev_a, i + 1 + FREE)
                sp.wait_ge(base.y_ev_d, i + 1 + FREE)
                sp.dma_start(rows_of(y_sorted, local), ysb[s]).then_inc(base.y_out[s], 16)

            extra = extras[l]

            def extra_loads(o):
                sp.dma_start(xe[0], rows_of(x_sorted, EPAIRS + o)).then_inc(extra.x_in[0], 16)
                for e in range(2):
                    expert = sp.value_load(over_expert[0:1, dyn(2 * o + e, 1)], min_val=0, max_val=EXPERTS - 1)
                    for w, src in enumerate((w_gate, w_up)):
                        sp.dma_start(wgu[0][:, w, e, :, :].rearrange("p c f -> p (c f)"),
                                     src[l, dyn(expert, 1)].rearrange("e (p c) f -> p (e c f)", c=C)).then_inc(extra.gu_in[0], 16)
                    sp.dma_start(wdn[0][:, e, :, :].rearrange("p c n -> p (c n)"),
                                 w_down[l, dyn(expert, 1)].rearrange("e (p c) n -> p (e c n)", c=FC)).then_inc(extra.dn_in[0], 16)

            def extra_store(o):
                sp.wait_ge(extra.y_ev_a, o + 1 + FREE)
                sp.wait_ge(extra.y_ev_d, o + 1 + FREE)
                sp.dma_start(rows_of(y_sorted, EPAIRS + o), ysb[0]).then_inc(extra.y_out[0], 16)
                sp.wait_ge(extra.y_out[0], 16 * (o + 1))
                sp.sem_inc(extra.y_free, 1)

            sp.sem_inc(extra.y_free, FREE)
            count = sp.value_load(over_count[0:1, 0:1], min_val=0, max_val=OPAIRS)
            with sp.Fori(0, EPAIRS // 2 - 1) as it:
                for s in range(2):
                    body(EPAIRS * l + 2 * it + s, s, 0, 2 * it + s, True)
            body(EPAIRS * (l + 1) - 2, 0, 0, EPAIRS - 2, True)
            with sp.If(count > 0):
                extra_loads(0)
            body(EPAIRS * (l + 1) - 1, 1, 0, EPAIRS - 1, False)
            for s in range(2):
                sp.wait_ge(base.y_out[s], 16 * (EPAIRS // 2) * (l + 1) + 16)
            with sp.If(count > 1):
                with sp.Fori(1, count) as o:
                    extra_store(o - 1)
                    extra_loads(o)
            with sp.If(count > 0):
                extra_store(count - 1)
            sp.sem_inc(extra_end, 1)

        def conv_sync(sp):
            wp1 = w_pw1[0].rearrange("(p c) n -> p c n", c=C)

            def load(cc, s):
                for w in range(2):
                    sp.dma_start(wp[s][:, w, :, :], wp1[:, :, dyn(w * D + cc * P, P)]).then_inc(wp_in[s], 16)

            for s in range(2):
                load(s, s)
            sp.dma_start(w2, w_pw2[0].rearrange("(c p) n -> p c n", p=P)).then_inc(w2_in, 16)
            sp.dma_start(raw[0:TAPS, :], w_dw[0]).then_inc(raw_in, 16)
            for n, row in enumerate((b_dw[0], ln_g[0], ln_b[0], b_pw1[0, 0:D], b_pw1[0, D:2 * D])):
                sp.dma_start(raw[TAPS + n:TAPS + n + 1, :], row.rearrange("(a n) -> a n", a=1)).then_inc(raw_in, 16)
            first_loads(sp, 1, 0)
            with sp.Fori(0, C // 2 - 1) as it:
                for s in range(2):
                    sp.wait_ge(glu_mm, 2 * it + s + 1)
                    load(2 * it + s + 2, s)

        def conv_small_pe(pe):
            pe.wait_ge(raw_in, 16 * 6)
            for c in range(C):
                mm = nc.tensor.transpose(bank[5][:, c * NV:(c + 1) * NV], raw[0:NV, c * P:(c + 1) * P], ident[0:NV, 0:NV])
            mm.then_inc(raw_mm, 1)
            pe.wait_ge(x_in, 48)
            for c in range(C):
                mm = nc.tensor.transpose(bank[6][:, c * STATE:(c + 1) * STATE], conv_cache[0:STATE, c * P:(c + 1) * P],
                                         ident[0:STATE, 0:STATE])
            mm.then_inc(raw_mm, 1)

        def conv_pe(pe):
            conv_small_pe(pe)
            pe.wait_ge(turn_ev_a, TILES * 3)
            pe.wait_ge(turn_ev_d, TILES * 3)

            def glu(n, s, k):
                pe.wait_ge(wp_in[s], 32 * (k + 1))
                pe.wait_ge(glu_done, n - 1 + CONV_LEAD)
                for w in range(2):
                    for c in range(C):
                        nc.tensor.matmul(bank[3 * s + w][:], wp[s][:, w, c, :], xt[:, c, 0:SEQ], start=c == 0, stop=c == C - 1)
                for w in range(2):
                    for c in range(C):
                        mm = nc.tensor.matmul(bank[3 * s + 2][:, w * DEC:(w + 1) * DEC], wp[s][:, w, c, :],
                                              xt[:, c, SEQ:TOKENS], start=c == 0, stop=c == C - 1)
                mm.then_inc(glu_mm, 1)

            def taps(n, s):
                pe.wait_ge(glu_done, n + 1 + CONV_LEAD)
                pe.wait_ge(diag_done, n + 1)
                pe.wait_ge(conv_done, n + CONV_LEAD)
                for b, at, m in ((6, 0, SEQ), (7, STATE + SEQ, DEC)):
                    for t in range(PE_TAPS):
                        mm = nc.tensor.matmul(bank[b][:, 0:m], diag[s][:, t, :], u[s][:, at + t:at + t + m],
                                              start=t == 0, stop=t == PE_TAPS - 1)
                mm.then_inc(conv_mm, 1)

            pe.wait_ge(raw_ev, 2)
            glu(0, 0, 0)
            with pe.Fori(0, C // 2 - 1) as it:
                for s in range(2):
                    glu(2 * it + s + 1, 1 - s, it + s)
                    taps(2 * it + s, s)
            glu(C - 1, 1, C // 2 - 1)
            for s in range(2):
                taps(C - 2 + s, s)
            pe.wait_ge(last_done, C + FREE)
            for c in range(C):
                mm = nc.tensor.transpose(bank[c // 4][0:2 * STATE, (c % 4) * P:(c % 4 + 1) * P], last_u[:, c, :], ident[:])
            mm.then_inc(last_mm, 1)
            pe.wait_ge(conv_done, C + CONV_LEAD)
            for c in range(C):
                nc.tensor.matmul(bank[5][:], mean_w[:], dw[:, c, 0:SEQ], start=c == 0, stop=c == C - 1)
            for c in range(C):
                mm = nc.tensor.matmul(bank[6][:, 0:DEC], mean_w[:], dw[:, c, SEQ:TOKENS], start=c == 0, stop=c == C - 1)
            mm.then_inc(mean_mm, 1)
            pe.wait_ge(sq_done, 1)
            for c in range(C):
                nc.tensor.matmul(bank[5][:], mean_w[:], sq[:, c * TOKENS:c * TOKENS + SEQ], start=c == 0, stop=c == C - 1)
            for c in range(C):
                mm = nc.tensor.matmul(bank[6][:, 0:DEC], mean_w[:], sq[:, c * TOKENS + SEQ:(c + 1) * TOKENS],
                                      start=c == 0, stop=c == C - 1)
            mm.then_inc(var_mm, 1)
            pe.wait_ge(swished, C)
            pe.wait_ge(w2_in, 16)
            project_pe(pe, 1, dw, w2)

        def conv_act(act, steps):
            act.wait_ge(raw_mm, 1)
            nc.scalar.copy(chan, bank[5][:, 0:C * NV].rearrange("p (c v) -> p c v", c=C)).then_inc(raw_ev, 1)
            act.wait_ge(raw_mm, 2)
            nc.scalar.copy(state, bank[6][:, 0:C * STATE].rearrange("p (c k) -> p c k", c=C)).then_inc(raw_ev, 1)
            act.wait_ge(raw_ev, 2)

            def fill(n, s):
                act.wait_ge(conv_done, n - 1 + CONV_LEAD)
                nc.scalar.copy(cvec[s], chan_flat[:, dyn(n * NV, NV)])
                nc.scalar.copy(u[s][:, STATE + SEQ:2 * STATE + SEQ],
                               state_flat[:, dyn(n * STATE, STATE)]).then_inc(u_filled, 1)

            def chunk(n, s):
                fill(n, s)
                act.wait_ge(u_filled, n + 1)
                for t in range(PE_TAPS):
                    ins = nc.scalar.activation(diag[s][:, t, :], ident[:], ACT.Copy, scale=cvec[s][:, t:t + 1])
                ins.then_inc(diag_done, 1)
                act.wait_ge(glu_mm, n + 1)
                act.wait_ge(glu_done, n + CONV_LEAD)
                g = cvec[s][:, TAPS + 4:TAPS + 5]
                nc.scalar.activation(sig[:, 0:SEQ], bank[3 * s + 1][:], ACT.Sigmoid, bias=g)
                nc.scalar.activation(sig[:, SEQ:TOKENS], bank[3 * s + 2][:, DEC:2 * DEC], ACT.Sigmoid, bias=g).then_inc(sig_done, 1)
                act.wait_ge(glu_done, n + 1 + CONV_LEAD)
                nc.scalar.copy(last_flat[:, dyn(2 * n * STATE, STATE)], u[s][:, SEQ:SEQ + STATE])
                nc.scalar.copy(last_flat[:, dyn((2 * n + 1) * STATE, STATE)], u[s][:, SPAN - STATE:SPAN]).then_inc(last_done, 1)

            with act.Fori(0, C // 2) as it:
                for s in range(2):
                    chunk(2 * it + s, s)
            act.wait_ge(last_mm, 1)
            for h in range(2):
                ins = nc.scalar.copy(last_rows[0:2 * STATE, h * HALF:(h + 1) * HALF], bank[h][0:2 * STATE, :])
            ins.then_inc(last_ev, 1)
            act.wait_ge(centred, 1)
            nc.scalar.activation(sq, dw_flat, ACT.Square).then_inc(sq_done, 1)
            act.wait_ge(var_ev, 1)
            nc.scalar.activation(sig[:], sig[:], ACT.Sqrt).then_inc(std_done, 1)
            act.wait_ge(scaled, 1)
            for c in range(C):
                nc.scalar.activation(dw[:, c, :], dw[:, c, :], ACT.Silu, bias=chan[:, c, TAPS + 2:TAPS + 3],
                                     scale=chan[:, c, TAPS + 1:TAPS + 2]).then_inc(swished, 1)

        CONV_LEAD = 2
        conv_cache = sb("conv_cache", [STATE, D])
        last_rows = raw

        def conv_dve(dve, steps):
            V = nc.vector
            dve.sem_inc(conv_done, CONV_LEAD)
            dve.sem_inc(glu_done, CONV_LEAD)
            for s in range(2):
                steps.done(V.memset(u[s][:, 0:STATE], 0.0))

            def gated(n, s):
                a = cvec[s][:, TAPS + 3:TAPS + 4]
                dve.wait_ge(u_filled, n + 1)
                dve.wait_ge(sig_done, n + 1)
                V.scalar_tensor_tensor(u[s][:, STATE:STATE + SEQ], bank[3 * s][:], a, sig[:, 0:SEQ], ALU.add, ALU.mult)
                V.scalar_tensor_tensor(u[s][:, SPAN - DEC:SPAN], bank[3 * s + 2][:, 0:DEC], a, sig[:, SEQ:TOKENS],
                                       ALU.add, ALU.mult).then_inc(glu_done, 1)
                dve.wait_ge(glu_done, n + 1 + CONV_LEAD)

            def taps(n, s):
                w = lambda t: cvec[s][:, t:t + 1]
                t = PE_TAPS
                steps.done(V.tensor_scalar(acc[s], u[s][:, t:t + OUTS], w(t), cvec[s][:, TAPS:TAPS + 1], ALU.mult, ALU.add))
                for t in range(PE_TAPS + 1, TAPS):
                    steps.done(V.scalar_tensor_tensor(acc[s], u[s][:, t:t + OUTS], w(t), acc[s], ALU.mult, ALU.add))

            def add(n, s):
                dve.wait_ge(conv_mm, n + 1)
                dve.wait_ge(last_done, n + FREE)
                V.tensor_tensor(xn_flat[:, dyn(n * TOKENS, SEQ)], bank[6][:], acc[s][:, 0:SEQ], ALU.add)
                V.tensor_tensor(xn_flat[:, dyn(n * TOKENS + SEQ, DEC)], bank[7][:, 0:DEC], acc[s][:, OUTS - DEC:OUTS],
                                ALU.add).then_inc(conv_done, 1)

            dve.wait_ge(raw_ev, 2)
            gated(0, 0)
            PER = 2 * (TAPS - PE_TAPS)
            with dve.Fori(0, C // 2 - 1) as it:
                steps.enter(it, PER)
                for s in range(2):
                    taps(2 * it + s, s)
                    gated(2 * it + s + 1, 1 - s)
                    add(2 * it + s, s)
            steps.leave(C // 2 - 1, PER)
            taps(C - 2, 0)
            gated(C - 1, 1)
            add(C - 2, 0)
            taps(C - 1, 1)
            add(C - 1, 1)
            dve.wait_ge(mean_mm, 1)
            V.tensor_tensor(dw[:, :, 0:SEQ], dw[:, :, 0:SEQ], bank[5][:].unsqueeze(1).to_broadcast([P, C, SEQ]), ALU.subtract)
            V.tensor_tensor(dw[:, :, SEQ:TOKENS], dw[:, :, SEQ:TOKENS],
                            bank[6][:, 0:DEC].unsqueeze(1).to_broadcast([P, C, DEC]), ALU.subtract).then_inc(centred, 1)
            dve.wait_ge(var_mm, 1)
            V.tensor_scalar(sig[:, 0:SEQ], bank[5][:], 1e-5, None, ALU.add)
            V.tensor_scalar(sig[:, SEQ:TOKENS], bank[6][:, 0:DEC], 1e-5, None, ALU.add).then_inc(var_ev, 1)
            dve.wait_ge(std_done, 1)
            steps.done(V.reciprocal(sig[:], sig[:]))
            V.tensor_tensor(dw, dw, sig[:].unsqueeze(1).to_broadcast([P, C, TOKENS]), ALU.mult).then_inc(scaled, 1)
            dve.wait_ge(gain_in, 16 * B_PW2_LOAD)
            project_dve(dve, steps, 1, gain[:, 0, :])

        CONSTS = 5

        block = ctx.enter_context(nc.Block())

        @block.sync
        def _(sp):
            xp = x_prompt[0].rearrange("(j p) d -> p j d", p=P)
            sp.dma_start(x[:, 0:TILES - 1, :], xp).then_inc(x_in, 16)
            sp.dma_start(x[0:DEC, TILES - 1, :], x_sample[0]).then_inc(x_in, 16)
            sp.dma_start(gain[:, 0, :], broadcast(norm_mix[0])).then_inc(gain_in, 16)
            attn_sync(sp)
            sp.dma_start(conv_cache[:], cache_conv[0, 0]).then_inc(x_in, 16)
            for l in range(LAYERS):
                sp.wait_ge(normed, TILES * (2 * l + 1))
                if l == 1:
                    sp.dma_start(gain[:, 0, :], broadcast(b_pw2[0])).then_inc(gain_in, 16)
                    conv_sync(sp)
                    sp.wait_ge(last_ev, 1)
                    sp.dma_start(cp_out[0, 0], last_rows[0:STATE, :]).then_inc(out_done, 16)
                    sp.dma_start(cs_out[0, 0], last_rows[STATE:2 * STATE, :]).then_inc(out_done, 16)
                    sp.wait_ge(proj_ev, 2 * TILES * 2)
                    sp.wait_ge(out_done, 32)
                sp.dma_start(gain[:, 0, :], broadcast(norm_ffn[l])).then_inc(gain_in, 16)
                for src, dst in ((w_group[l], router_w[:, :, 0:GROUPS]), (w_router[l], router_w[:, :, GROUPS:RC])):
                    sp.dma_start(dst, src.rearrange("(p c) n -> p c n", c=C)).then_inc(small_in, 16)
                for src, dst in ((b_group[l], router_b[:, 0:GROUPS]), (b_router[l], router_b[:, GROUPS:RC])):
                    sp.dma_start(dst, broadcast(src)).then_inc(small_in, 16)
                if l == 0:
                    first_loads(sp, l, 0)
                first_loads(sp, l, 1)
                experts_sync(sp, l)
                sp.dma_start(gain[:, 0, :], broadcast(norm_mix[l + 1] if l + 1 < LAYERS else norm_final)).then_inc(gain_in, 16)
            for j in range(TILES):
                sp.wait_ge(normed, TILES * 2 * LAYERS + j + 1)
                dst = y_prompt[0, j * P:(j + 1) * P, :] if j < TILES - 1 else y_sample[0]
                sp.dma_start(dst, xn[0:rows[j], j, :]).then_inc(out_done, 16)
            sp.wait_ge(out_done, 16 * (TILES + 2))

        @block.gpsimd
        def _(pool):
            steps = Steps(pool, pool_steps)
            for t, fill, cmp, pat, mult, b in ((ident, 1.0, ALU.not_equal, [[-1, P]], 1, 0),):
                steps.done(pool.memset(t[:], 0.0))
                pool.affine_select(out=t[:], in_=t[:], compare_op=cmp, fill=fill, base=b, pattern=pat,
                                   channel_multiplier=mult).then_inc(ident0, 1)
            steps.done(pool.memset(ones[:], 1.0))
            steps.done(pool.affine_select(out=lower[:], in_=ones[:], compare_op=ALU.is_gt, fill=0.0, base=0,
                                          pattern=[[1, P]], channel_multiplier=-1))
            steps.done(pool.memset(mean_w[:], 1.0 / D))
            steps.done(pool.memset(gain[:, 1, :], 0.0))
            for s in range(2):
                steps.done(pool.memset(qz[s][HD:P, 0, :], 0.0))
                steps.done(pool.memset(qz[s][0:HD, 1, :], 0.0))
            steps.done(pool.memset(logits[:], 0.0))
            steps.done(pool.memset(ss[:], 1.0))
            steps.done(pool.iota(down_i[:], [[-1, EXPERTS]], base=EXPERTS, channel_multiplier=0))
            steps.done(pool.iota(up_i[:], [[1, OVER + EXPERTS]], base=0, channel_multiplier=0))
            steps.done(pool.tensor_copy(down_iota[:], down_i[:]))
            steps.done(pool.tensor_copy(up_iota[:], up_i[:, 0:EXPERTS]))
            steps.done(pool.tensor_copy(orow[:], up_i[:, 0:OVER]))
            pool.sem_inc(consts, CONSTS)
            pool.dma_start(heads2d(ks_out[0, 0])[0:KEEP - DEC, :], heads2d(cache_attn_k[0, 0])[DEC:KEEP, :]).then_inc(kv_out[0], 16)
            pool.dma_start(heads2d(vs_out[0, 0])[0:KEEP - DEC, :], heads2d(cache_attn_v[0, 0])[DEC:KEEP, :]).then_inc(kv_out[1], 16)
            attn_pool(pool)
            for l in range(LAYERS):
                scatter_pool(pool, l)
                gather_pool(pool, l)

        @block.scalar
        def _(act):
            steps = Steps(act, act_steps)
            act.wait_ge(consts, CONSTS)
            norm_act(act, steps, 0)
            turn_act(act, 0)
            attn_act(act, steps)
            for l in range(LAYERS):
                if l == 1:
                    norm_act(act, steps, 2 * l)
                    turn_act(act, 2 * l)
                    conv_act(act, steps)
                norm_act(act, steps, 2 * l + 1)
                turn_act(act, 2 * l + 1)
                router_act(act, l)
                experts_act(act, l)
            norm_act(act, steps, 2 * LAYERS)

        @block.vector
        def _(dve):
            steps = Steps(dve, dve_steps)
            dve.wait_ge(rel_in, 16)
            V = nc.vector
            V.tensor_copy(rel_sb[0:HEADS, 0:P - 1], rel_sb[0:HEADS, P - 1:P].to_broadcast([HEADS, P - 1])).then_inc(rel_ext, 1)
            dve.wait_ge(consts, CONSTS)
            norm_dve(dve, steps, 0)
            turn_dve(dve, 0)
            attn_dve(dve, steps)
            project_dve(dve, steps, 0, None)
            for l in range(LAYERS):
                if l == 1:
                    norm_dve(dve, steps, 2 * l)
                    turn_dve(dve, 2 * l)
                    conv_dve(dve, steps)
                norm_dve(dve, steps, 2 * l + 1)
                turn_dve(dve, 2 * l + 1)
                router_dve(dve, steps, l)
                experts_dve(dve, l)
                combine_dve(dve, steps, l)
            norm_dve(dve, steps, 2 * LAYERS)

        @block.tensor
        def _(pe):
            pe.wait_ge(ident0, 1)
            turn_pe(pe, 0)
            attn_pe(pe)
            pe.wait_ge(wo_in, 16)
            pe.wait_ge(op_ev, PAIRS + FREE)
            pe.wait_ge(os_ev, PAIRS)
            project_pe(pe, 0, ot, wo_sb)
            for l in range(LAYERS):
                if l == 1:
                    turn_pe(pe, 2 * l)
                    conv_pe(pe)
                turn_pe(pe, 2 * l + 1)
                router_pe(pe, l)
                experts_pe(pe, l)


_INS = ['x_prompt', 'x_sample', 'cache_attn_k', 'cache_attn_v', 'cache_conv', 'norm_mix', 'norm_ffn', 'norm_final',
        'w_qkv', 'w_o', 'rel_table', 'w_pw1', 'b_pw1', 'w_dw', 'b_dw', 'ln_g', 'ln_b', 'w_pw2', 'b_pw2',
        'w_group', 'b_group', 'w_router', 'b_router', 'w_gate', 'w_up', 'w_down']


def kernel(**inputs):
    import numpy as _np
    import concourse.bacc as _bacc
    from concourse.bass_utils import run_bass_kernel_spmd as _run

    shapes = {k: tuple(v.shape) for k, v in inputs.items()}
    kv = (shapes['cache_attn_k'][0], shapes['x_prompt'][0]) + shapes['cache_attn_k'][2:]
    conv = (shapes['cache_conv'][0], shapes['x_prompt'][0]) + shapes['cache_conv'][2:]
    outs = [shapes['x_prompt'], shapes['x_sample'], kv, kv, conv,
            shapes['cache_attn_k'], shapes['cache_attn_v'], shapes['cache_conv']]
    nc = _bacc.Bacc("TRN2", target_bir_lowering=False, num_devices=1)
    arrays, args = {}, []
    for name in _INS:
        a = _np.asarray(inputs[name])
        if name == 'rel_table':
            a = a[:, :, ::-1]
        a = _np.ascontiguousarray(a)
        arrays[f"in_{name}"] = a
        args.append(nc.dram_tensor(f"in_{name}", a.shape, mybir.dt.from_np(a.dtype), kind="ExternalInput").ap())
    for i, shape in enumerate(outs):
        args.append(nc.dram_tensor(f"out_{i}", shape, F32, kind="ExternalOutput").ap())
    encoder(nc, *args)
    r = _run(nc, [arrays], core_ids=[0])
    return tuple(r.results[0][f"out_{i}"] for i in range(len(outs)))
```

```python
from contextlib import ExitStack

import concourse.bass as bass
from concourse import mybir

F32 = mybir.dt.float32
I32 = mybir.dt.int32
ALU = mybir.AluOpType
ACT = mybir.ActivationFunctionType
AX = mybir.AxisListType

P = 128
ROWS64 = 64
BIG = 3.0e38


class Steps:

    def __init__(self, engine, sem):
        self.engine, self.sem, self.base, self.count = engine, sem, 0, 0

    def done(self, instruction):
        instruction.then_inc(self.sem, 1)
        self.count += 1
        self.engine.wait_ge(self.sem, self.base + self.count)

    def enter(self, turn, per_turn):
        self.base, self.start = turn * per_turn + self.count, self.count
        self.count = 0

    def leave(self, turns, per_turn):
        assert self.count == per_turn, self.count
        self.base, self.count = 0, self.start + turns * per_turn


def encoder(nc, x_prompt, x_sample, cache_attn_k, cache_attn_v, cache_conv,
            norm_mix, norm_ffn, norm_final, w_qkv, w_o, rel_rev,
            w_pw1, b_pw1, w_dw, b_dw, ln_g, ln_b, w_pw2, b_pw2,
            w_group, b_group, w_router, b_router, w_gate, w_up, w_down,
            y_prompt, y_sample, kp_out, vp_out, cp_out, ks_out, vs_out, cs_out):
    SEQ, D = x_prompt.shape[1:]
    DEC = x_sample.shape[1]
    TOKENS = SEQ + DEC
    TILES = SEQ // P + 1
    rows = [P] * (TILES - 1) + [DEC]
    C = D // P
    KEEP, HEADS, HD = cache_attn_k.shape[2:]
    PAIRS = HEADS // 2
    NREL = rel_rev.shape[2]
    CHUNK = ROWS64
    TAPS = w_dw.shape[1]
    STATE = TAPS - 1
    GROUPS = w_group.shape[2]
    EXPERTS = w_router.shape[2]
    PER_GROUP = EXPERTS // GROUPS
    FE = w_gate.shape[3]
    FC = FE // P
    LAYERS = w_gate.shape[0]
    HALF = D // 2
    CAP = P // 2
    EPAIRS = EXPERTS // 2
    MAXQ = (TOKENS - 1) // CAP
    OVER = 2 * ((2 * TOKENS // CAP + 1) // 2)
    OPAIRS = OVER // 2
    RC = GROUPS + EXPERTS
    assert HD == CHUNK == DEC and HEADS * HD == D and KEEP == P and C == 8 and FC == 2
    SCALE = float(HD) ** -0.5
    KCOLS = SEQ + KEEP + DEC
    WIN = 2 * P
    EXT = P - 1 + WIN
    SPAN = STATE + SEQ + STATE + DEC
    OUTS = SPAN - STATE
    UNITS = 2 * TILES

    with ExitStack() as ctx:
        def sb(name, shape, dt=F32):
            return ctx.enter_context(nc.sbuf_tensor(name, shape, dt))

        def sem(name):
            return ctx.enter_context(nc.semaphore(name))

        bank = [ctx.enter_context(nc.psum_tensor(f"bank{i}", [P, 512], F32)) for i in range(8)]

        bias_rows = nc.dram_tensor("bias_rows", [P, HEADS, EXT], F32).ap()
        SLOTS = (EXPERTS + OVER) * CAP
        x_sorted = nc.dram_tensor("x_sorted", [SLOTS, D], F32).ap()
        y_sorted = nc.dram_tensor("y_sorted", [SLOTS, D], F32).ap()

        x = sb("x", [P, TILES, D])
        xn_flat = sb("xn_flat", [P, TILES * D])
        xt_flat = sb("xt_flat", [P, TILES * D])
        ring = sb("ring", [P, 2, 2 * 3 * C * FE])
        work = sb("work", [P, 5952])
        gain = sb("gain", [P, 2, D])
        ident = sb("ident", [P, P])
        ones = sb("ones", [P, P])
        lower = sb("lower", [P, P])
        mean_w = sb("mean_w", [P, P])
        router_w = sb("router_w", [P, C, RC])
        router_b = sb("router_b", [P, RC])
        logits = sb("logits", [P, TILES, RC])
        ss = sb("ss", [P, 3, TILES])
        eps = sb("eps", [P, 1])
        ln_eps = sb("ln_eps", [P, 1])
        cand = sb("cand", [P, EXPERTS])
        pen = sb("pen", [P, GROUPS])
        held = sb("held", [P, 2, EXPERTS])
        hot = sb("hot", [P, 2, TILES, EXPERTS])
        picked = sb("picked", [P, TILES, EXPERTS])
        tok = sb("tok", [P, 11, TILES])
        gexp = sb("gexp", [P, TILES, GROUPS])
        down_iota = sb("down_iota", [P, EXPERTS])
        first_row = sb("first_row", [P, EXPERTS])
        more_row = sb("more_row", [P, EXPERTS])
        qrow = sb("qrow", [P, MAXQ])
        qcmp = sb("qcmp", [P, EXPERTS, MAXQ])
        zero_e = sb("zero_e", [P, EXPERTS])
        more_tiles = sb("more_tiles", [P, EXPERTS])
        ends = sb("ends", [P, 1 + EXPERTS])
        shift = sb("shift", [P, EXPERTS])
        place = sb("place", [P, 2, TILES, EXPERTS])
        at_slot = sb("at_slot", [P, 2, TILES, EXPERTS])
        slot_f = sb("slot_f", [P, 2, TILES])
        orow = sb("orow", [P, OVER])
        ocmp = sb("ocmp", [P, OVER, EXPERTS])
        oexp = sb("oexp", [P, OVER])
        ofew = sb("ofew", [P, OPAIRS])
        opairs = sb("opairs", [P, 1])
        over_expert = sb("over_expert", [P, OVER], I32)
        over_count = sb("over_count", [P, 1], I32)
        down_i = sb("down_i", [P, EXPERTS], I32)
        up_i = sb("up_i", [P, OVER + EXPERTS], I32)
        slot = sb("slot", [P, 2, TILES], I32)
        gate_w = sb("gate_w", [P, 2, TILES])
        soft = sb("soft", [P, 3, 5])

        xn = xn_flat[:].rearrange("p (j d) -> p j d", j=TILES)
        xn_cp = xn_flat[:].rearrange("p (j c q) -> p j q c", j=TILES, c=C)
        xt = xt_flat[:, 0:C * TOKENS].rearrange("p (c t) -> p c t", c=C)
        xf = xt_flat[:].rearrange("p (j d) -> p j d", j=TILES)
        xf_cp = xt_flat[:].rearrange("p (j c q) -> p j q c", j=TILES, c=C)
        xw = work[:, 0:C * TOKENS].rearrange("p (c t) -> p c t", c=C)
        junk = work[:, C * TOKENS:C * TOKENS + D]
        yg = ring[:, 1, 0:TILES * D].rearrange("p (j d) -> p j d", j=TILES)

        def cut(flat, sizes):
            out, at = [], 0
            for n in sizes:
                out.append(flat[:, at:at + n])
                at += n
            assert at <= flat.shape[1], (at, flat.shape)
            return out

        W3 = 3 * C * P
        part = cut(ring[:, 0, :], [W3, W3] + [2 * TOKENS, KCOLS, (TILES + 1) * P] * 2)
        wa = [part[s].rearrange("p (w c n) -> p w c n", w=3, c=C) for s in range(2)]
        qz = [part[2 + 3 * s].rearrange("p (h t) -> p h t", h=2) for s in range(2)]
        kt = [part[3 + 3 * s] for s in range(2)]
        vv = [part[4 + 3 * s].rearrange("p (j n) -> p j n", j=TILES + 1) for s in range(2)]
        part = cut(ring[:, 1, :], [C * D, HEADS * WIN])
        bias_flat = part[1]
        bias = part[1].rearrange("p (h m) -> p h m", h=HEADS)
        wo_sb = part[0].rearrange("p (c n) -> p c n", c=C)
        part = cut(work[:], [5 * SEQ, 2 * SEQ, 2 * 2 * P, 2 * P, EXT + 1])
        prob = part[0].rearrange("p (b k) -> p b k", b=5)
        pt = part[1].rearrange("p (b k) -> p b k", b=2)
        k_rows = part[2].rearrange("p (s w n) -> p s w n", s=2, w=2)
        kcache = part[3].rearrange("p (s n) -> p s n", s=2)
        rel_sb = part[4]
        ot = xn_flat[:, 0:C * TOKENS].rearrange("p (c t) -> p c t", c=C)

        wgu = [ring[:, s, 0:4 * C * FE].rearrange("p (w e c f) -> p w e c f", w=2, e=2, c=C) for s in range(2)]
        wdn = [ring[:, s, 4 * C * FE:6 * C * FE].rearrange("p (e c n) -> p e c n", e=2, c=FC) for s in range(2)]
        part = cut(work[:], [D, D, D, D, FE, FE, FE, D])
        xe = part[0:2]
        xte = [a.rearrange("p (c r) -> p c r", c=C) for a in part[2:4]]
        sg, hid, hts = part[4], part[5], part[6].rearrange("p (c r) -> p c r", c=FC)
        hid_cp = hid.rearrange("p (c q) -> p q c", c=FC)
        ysb = [part[7], gain[:, 1, :]]

        part = cut(work[:], [2 * C * P, 2 * C * P, SPAN, SPAN, TOKENS])
        wp = [part[s].rearrange("p (w c n) -> p w c n", w=2, c=C) for s in range(2)]
        u = part[2:4]
        sig = part[4]
        dw_flat = xn_flat[:, 0:C * TOKENS]
        dw = dw_flat.rearrange("p (c t) -> p c t", c=C)
        w2 = ring[:, 1, 0:C * D].rearrange("p (c n) -> p c n", c=C)
        NV = TAPS + 5
        rest = ring[:, 1, C * D:]
        PE_TAPS = 6
        part = cut(rest, [C * NV, C * STATE, NV, NV, C * 2 * STATE, OUTS, OUTS, PE_TAPS * P, PE_TAPS * P])
        chan_flat, state_flat, last_flat = part[0], part[1], part[4]
        chan = part[0].rearrange("p (c v) -> p c v", c=C)
        state = part[1].rearrange("p (c k) -> p c k", c=C)
        cvec = part[2:4]
        last_u = part[4].rearrange("p (c k) -> p c k", c=C)
        acc = part[5:7]
        acc_at = C * NV + C * STATE + 2 * NV + C * 2 * STATE
        b2 = rest[:, acc_at:acc_at + D]
        diag = [a.rearrange("p (t q) -> p t q", t=PE_TAPS) for a in part[7:9]]
        raw = gain[:, 1, :]
        sq = xt_flat[:, 0:C * TOKENS].rearrange("p (c t) -> p c t", c=C)

        x_in = [sem(f"x_in{j}") for j in range(TILES)]; cache_in = sem("cache_in"); small_in = sem("small_in"); gain_in = sem("gain_in"); consts = sem("consts")
        ident0 = sem("ident0")
        rel_in = sem("rel_in"); rel_ext = sem("rel_ext"); rel_out = sem("rel_out"); bias_in = sem("bias_in")
        bias_masked = sem("bias_masked"); zeros_in = sem("zeros_in"); wo_in = sem("wo_in")
        rooted = sem("rooted"); normed = sem("normed")
        turned = sem("turned"); turn_ev_a = sem("turn_ev_a"); turn_ev_d = sem("turn_ev_d")
        dve_steps = sem("dve_steps"); act_steps = sem("act_steps"); pool_steps = sem("pool_steps")
        wa_in = [sem(f"wa_in{s}") for s in range(2)]; vc_in = [sem(f"vc_in{s}") for s in range(2)]
        q_mm = sem("q_mm"); k_mm = sem("k_mm"); small_mm = sem("small_mm"); v_mm = sem("v_mm"); v4_mm = sem("v4_mm")
        q_ev = sem("q_ev"); k_ev = sem("k_ev"); small_ev = sem("small_ev"); v_ev = sem("v_ev"); v4_ev = sem("v4_ev")
        score_mm = sem("score_mm"); score_free = sem("score_free"); maxed = sem("maxed"); exped = sem("exped")
        probs = sem("probs"); pt_mm = sem("pt_mm"); pt_ev = sem("pt_ev"); os_mm = sem("os_mm"); os_ev = sem("os_ev")
        op_mm = sem("op_mm"); op_ev = sem("op_ev"); krow_mm = sem("krow_mm"); krow_ev = sem("krow_ev")
        kv_out = [sem(f"kv_out{s}") for s in range(2)]
        proj_mm = sem("proj_mm"); proj_ev = sem("proj_ev")
        route_mm = sem("route_mm"); gates_max = sem("gates_max"); gates_exp = sem("gates_exp")
        second = sem("second"); second_exp = sem("second_exp"); picks = sem("picks"); ranks = sem("ranks")
        routed = sem("routed"); further_known = sem("further_known"); b2_in = sem("b2_in")
        scattered = sem("scattered"); gathered = [sem(f"gathered{j}") for j in range(TILES)]
        combined = sem("combined")

        class ExpertSems:

            def __init__(self, tag, slots=2):
                two = lambda n: [sem(f"{tag}_{n}{s}") for s in range(slots)]
                self.y_free = sem(f"{tag}_y_free") if slots == 1 else None
                self.x_in, self.gu_in, self.dn_in, self.y_out = two("x_in"), two("gu_in"), two("dn_in"), two("y_out")
                (self.xt_mm, self.xt_ev_a, self.xt_ev_d, self.gu_mm, self.silu, self.hid, self.ht_mm, self.ht_ev,
                 self.dn_mm, self.y_ev_a, self.y_ev_d) = (
                    sem(f"{tag}_{n}") for n in ("xt_mm", "xt_ev_a", "xt_ev_d", "gu_mm", "silu", "hid", "ht_mm", "ht_ev",
                                                "dn_mm", "y_ev_a", "y_ev_d"))

        base = ExpertSems("ex")
        extras = [ExpertSems(f"ov{l}", 1) for l in range(LAYERS)]
        extra_end = sem("extra_end")
        raw_in = sem("raw_in"); raw_mm = sem("raw_mm"); raw_ev = sem("raw_ev")
        wp_in = [sem(f"wp_in{s}") for s in range(2)]; w2_in = sem("w2_in")
        glu_mm = sem("glu_mm"); sig_done = sem("sig_done"); glu_done = sem("glu_done"); cvec_done = sem("cvec_done")
        u_filled = sem("u_filled"); last_done = sem("last_done"); conv_done = sem("conv_done"); diag_done = sem("diag_done"); conv_mm = sem("conv_mm")
        last_mm = sem("last_mm"); last_ev = sem("last_ev")
        mean_mm = sem("mean_mm"); centred = sem("centred"); sq_done = sem("sq_done"); var_mm = sem("var_mm")
        var_ev = sem("var_ev"); std_done = sem("std_done"); scaled = sem("scaled"); swished = sem("swished")
        y_ready = sem("y_ready"); out_done = sem("out_done")

        dyn = bass.ds
        FREE = 1

        def norm_act(act, steps, n, j):
            r = rows[j]
            wait_x(act, n, j)
            out = junk[0:r, :] if n % 2 else xn[0:r, j, :]
            steps.done(nc.scalar.activation(out, x[0:r, j, :], ACT.Square, accum_out=ss[0:r, 0, j:j + 1]))
            nc.scalar.activation(ss[0:r, 1, j:j + 1], ss[0:r, 0, j:j + 1], ACT.Sqrt, bias=eps[0:r, :],
                                 scale=1.0 / D).then_inc(rooted, 1)

        def norm_dve(dve, steps, n, j):
            r = rows[j]
            dve.wait_ge(rooted, TILES * n + j + 1)
            steps.done(nc.vector.reciprocal(ss[0:r, 2, j:j + 1], ss[0:r, 1, j:j + 1]))
            if j == 0:
                dve.wait_ge(gain_in, 16 * (n + 1))
            wait_x(dve, n, j)
            final = n == 2 * LAYERS
            out = xn[0:r, j, :] if final else (xf_cp if n % 2 else xn_cp)[0:r, j, :, :]
            src = x[0:r, j, :] if final else x[0:r, j, :].rearrange("p (q c) -> p q c", c=C)
            g = gain[0:r, 0, :] if final else gain[0:r, 0, :].rearrange("p (q c) -> p q c", c=C)
            nc.vector.scalar_tensor_tensor(out, src, ss[0:r, 2, j:j + 1], g, ALU.mult, ALU.mult).then_inc(normed, 1)

        TURN_BANKS = ((0, 1), (2, 7))

        def turn_pe(pe, n, j):
            r, at = rows[j], TILES * n + j
            pe.wait_ge(normed, at + 1)
            if at >= 2:
                pe.wait_ge(turn_ev_a, at - 1)
                pe.wait_ge(turn_ev_d, at - 1)
            src = xf if n % 2 else xn
            for c in range(C):
                b = bank[TURN_BANKS[at % 2][c // 4]]
                mm = nc.tensor.transpose(b[:, (c % 4) * P:(c % 4) * P + r], src[0:r, j, c * P:(c + 1) * P],
                                         ident[0:r, 0:r])
            mm.then_inc(turned, 1)

        def turn_copy(eng, copy, n, j, half, done):
            r, at = rows[j], TILES * n + j
            if n == 1 and j == 0:
                for s in range(2):
                    eng.wait_ge(kv_out[s], 64 * PAIRS // 2 + 16)
            eng.wait_ge(turned, at + 1)
            src = bank[TURN_BANKS[at % 2][half]][:].rearrange("p (c t) -> p c t", c=4)
            dst = xw if n % 2 else xt
            copy(dst[:, 4 * half:4 * half + 4, j * P:j * P + r], src[:, :, 0:r]).then_inc(done, 1)

        def turn_act(act, n, j):
            turn_copy(act, nc.scalar.copy, n, j, 0, turn_ev_a)

        def turn_dve(dve, n, j):
            turn_copy(dve, nc.vector.tensor_copy, n, j, 1, turn_ev_d)

        def norms_pe(pe, n):
            for j in range(TILES):
                turn_pe(pe, n, j)

        def norms_act(act, steps, n):
            for j in range(TILES + 1):
                if j >= 1 and n % 2:
                    turn_act(act, n, j - 1)
                if j < TILES:
                    norm_act(act, steps, n, j)
                if j >= 1 and n % 2 == 0 and n < 2 * LAYERS:
                    turn_act(act, n, j - 1)

        def norms_dve(dve, steps, n):
            for j in range(TILES + 2):
                if n > 0 and j < TILES:
                    combine_dve(dve, steps, n // 2 - 1, j)
                if 1 <= j <= TILES:
                    norm_dve(dve, steps, n, j - 1)
                if j >= 2 and n < 2 * LAYERS:
                    turn_dve(dve, n, j - 2)

        def wait_x(eng, n, j):
            if n == 0:
                eng.wait_ge(x_in[j], 16)
            elif n % 2:
                eng.wait_ge(proj_ev, 2 * TILES * (n // 2) + 2 * (j + 1))
            else:
                eng.wait_ge(combined, TILES * (n // 2 - 1) + j + 1)

        def broadcast(row):
            return bass.AP(row.tensor, row.offset, [[0, P], [1, row.shape[-1]]])

        def xt_tile(c, j):
            return xt[:, c, j * P:j * P + rows[j]]

        def project_pe(pe, l, act_t, w, ready):
            def half(j, h, between):
                at = 2 * TILES * l + 2 * j + h
                if 2 * j + h >= 2:
                    pe.wait_ge(proj_ev, at - 1)
                for c in range(C):
                    if c == C // 2:
                        between()
                    if ready is not None and j == h == 0:
                        pe.wait_ge(ready, c + 1)
                    mm = nc.tensor.matmul(bank[3 + h][0:rows[j], :], act_t[:, c, j * P:j * P + rows[j]],
                                          w[:, c, h * HALF:(h + 1) * HALF], start=c == 0, stop=c == C - 1)
                mm.then_inc(proj_mm, 1)

            for j in range(TILES):
                half(j, 0, lambda: None)
                if j >= 1:
                    turn_pe(pe, 2 * l + 1, j - 1)
                half(j, 1, lambda: logits_pe(pe, l, j - 1) if j >= 1 else None)
                if j >= 1:
                    ranks_pe(pe, l, j - 1)
            turn_pe(pe, 2 * l + 1, TILES - 1)
            logits_pe(pe, l, TILES - 1)
            ranks_pe(pe, l, TILES - 1)

        def project_dve(dve, steps, l, bias_row):
            def add(j, h):
                dve.wait_ge(proj_mm, 2 * TILES * l + 2 * j + h + 1)
                r, cols = rows[j], slice(h * HALF, (h + 1) * HALF)
                nc.vector.tensor_tensor(x[0:r, j, cols], x[0:r, j, cols], bank[3 + h][0:r, :], ALU.add).then_inc(proj_ev, 1)

            for j in range(TILES):
                if bias_row is not None:
                    r = rows[j]
                    steps.done(nc.vector.tensor_tensor(x[0:r, j, :], x[0:r, j, :], bias_row[0:r, :], ALU.add))
                add(j, 0)
                if j >= 1:
                    turn_dve(dve, 2 * l + 1, j - 1)
                    choose_dve(dve, steps, l, j - 1)
                add(j, 1)
                norm_dve(dve, steps, 2 * l + 1, j)
            turn_dve(dve, 2 * l + 1, TILES - 1)
            choose_dve(dve, steps, l, TILES - 1)

        def unit(uu):
            h, i = uu % 2, uu // 2 - 1
            if i < 0:
                return h, None, DEC, KEEP + DEC
            return h, i, P, (i + 1) * P

        PT_LEAD = 5
        SC_LEAD = 2

        def attn_pe(pe):
            def project(n, s, k, step):
                if step == 0:
                    pe.wait_ge(wa_in[s], 64 * (k + 1))
                    pe.wait_ge(v_ev, n)
                    for c in range(C):
                        mm = nc.tensor.matmul(bank[0][:], wa[s][:, 0, c, :], xt[:, c, 0:SEQ], start=c == 0, stop=c == C - 1)
                    mm.then_inc(q_mm, 1)
                if step == 1:
                    pe.wait_ge(v4_ev, n)
                    for c in range(C):
                        mm = nc.tensor.matmul(bank[1][:], wa[s][:, 1, c, :], xt[:, c, 0:SEQ], start=c == 0, stop=c == C - 1)
                    mm.then_inc(k_mm, 1)
                if step == 2:
                    pe.wait_ge(os_ev, n)
                    pe.wait_ge(krow_ev, n)
                    for w in range(2):
                        for c in range(C):
                            nc.tensor.matmul(bank[2][:, w * DEC:(w + 1) * DEC], wa[s][:, w, c, :], xt[:, c, SEQ:TOKENS],
                                             start=c == 0, stop=c == C - 1)
                    nc.tensor.transpose(bank[2][:, P:2 * P], kcache[:, s, :], ident[:, :]).then_inc(small_mm, 1)
                if step == 3:
                    pe.wait_ge(q_ev, n + 1)
                    for j in range(TILES - 1):
                        for c in range(C):
                            mm = nc.tensor.matmul(bank[0][:, j * P:(j + 1) * P], xt_tile(c, j), wa[s][:, 2, c, :],
                                                  start=c == 0, stop=c == C - 1)
                    mm.then_inc(v_mm, 1)
                if step == 4:
                    pe.wait_ge(k_ev, n + 1)
                    for c in range(C):
                        mm = nc.tensor.matmul(bank[1][0:DEC, 0:P], xt_tile(c, TILES - 1), wa[s][:, 2, c, :],
                                              start=c == 0, stop=c == C - 1)
                    mm.then_inc(v4_mm, 1)

            def scores(n, s, uu):
                h, i, q, nk = unit(uu)
                g = n * UNITS + uu
                if uu == 0:
                    pe.wait_ge(q_ev, n + 1)
                    pe.wait_ge(k_ev, n + 1)
                    pe.wait_ge(small_ev, n + 1)
                pe.wait_ge(score_free, g - 1 + SC_LEAD)
                q0 = SEQ if i is None else i * P
                k0 = SEQ if i is None else 0
                nc.tensor.matmul(bank[3 + uu % 2][0:q, 0:nk], qz[s][:, h, q0:q0 + q], kt[s][:, k0:k0 + nk],
                                 start=True, stop=True).then_inc(score_mm, 1)

            def turn(n, s, uu):
                h, i, q, nk = unit(uu)
                g = n * UNITS + uu
                pe.wait_ge(probs, g + 1)
                pe.wait_ge(pt_ev, g - 1 + PT_LEAD)
                b = bank[5 + uu % 2]
                for j in range((nk + P - 1) // P):
                    m = min(P, nk - j * P)
                    if i is None and j == 0:
                        nc.tensor.matmul(b[0:m, 0:q], prob[0:q, uu % 5, 0:m], ident[0:q, 0:q], start=True, stop=True)
                        continue
                    mm = nc.tensor.transpose(b[0:m, j * q:(j + 1) * q], prob[0:q, uu % 5, j * P:j * P + m], ident[0:q, 0:q])
                mm.then_inc(pt_mm, 1)

            def values(n, s, k, uu):
                h, i, q, nk = unit(uu)
                g = n * UNITS + uu
                pe.wait_ge(pt_ev, g + 1 + PT_LEAD)
                if uu == 0:
                    pe.wait_ge(v_ev, n + 1)
                    pe.wait_ge(v4_ev, n + 1)
                    pe.wait_ge(vc_in[s], 16 * (k + 1))
                hd = slice(h * HD, (h + 1) * HD)
                if i is None:
                    nc.tensor.matmul(bank[2][hd, 0:DEC], vv[s][:, TILES, hd], pt[:, uu % 2, 0:DEC], start=True, stop=False)
                    mm = nc.tensor.matmul(bank[2][hd, 0:DEC], vv[s][0:DEC, TILES - 1, hd], pt[0:DEC, uu % 2, DEC:2 * DEC],
                                          start=False, stop=True)
                    if uu == 1:
                        mm.then_inc(os_mm, 1)
                    return
                if uu == 2:
                    pe.wait_ge(op_ev, n + FREE)
                for j in range(i + 1):
                    mm = nc.tensor.matmul(bank[7][hd, i * P:(i + 1) * P], vv[s][:, j, hd], pt[:, uu % 2, j * P:(j + 1) * P],
                                          start=j == 0, stop=j == i)
                if uu == UNITS - 1:
                    mm.then_inc(op_mm, 1)

            def key_rows(n, s):
                pe.wait_ge(os_ev, n + 1)
                nc.tensor.transpose(bank[2][:, 0:P], kt[s][:, SEQ - KEEP:SEQ], ident[:, :])
                nc.tensor.transpose(bank[2][0:DEC, P:2 * P], kt[s][:, SEQ + KEEP:KCOLS], ident[:, :]).then_inc(krow_mm, 1)

            def pair(n, s, k, more):
                s2, k2 = (s + 1) % 2, k + (s + 1) // 2
                scores(n, s, 0)
                scores(n, s, 1)
                if more:
                    project(n + 1, s2, k2, 0)
                for uu in range(UNITS):
                    if uu + 2 < UNITS:
                        scores(n, s, uu + 2)
                    turn(n, s, uu)
                    if uu >= 1:
                        values(n, s, k, uu - 1)
                    if uu == 2 and more:
                        project(n + 1, s2, k2, 1)
                    if uu == 4:
                        key_rows(n, s)
                    if uu == 6 and more:
                        project(n + 1, s2, k2, 2)
                    if uu == 7 and more:
                        project(n + 1, s2, k2, 3)
                    if uu == 9 and more:
                        project(n + 1, s2, k2, 4)
                values(n, s, k, UNITS - 1)

            pe.wait_ge(turn_ev_a, TILES)
            pe.wait_ge(turn_ev_d, TILES)
            pe.wait_ge(consts, CONSTS)
            for step in range(5):
                project(0, 0, 0, step)
            with pe.Fori(0, PAIRS // 2 - 1) as it:
                for s in range(2):
                    pair(2 * it + s, s, it, True)
            for s in range(2):
                pair(PAIRS - 2 + s, s, PAIRS // 2 - 1, s == 0)

        def attn_act(act, steps):
            def query_copy(n, s):
                act.wait_ge(q_mm, n + 1)
                for h in range(2):
                    hd = slice(h * HD, (h + 1) * HD)
                    ins = nc.scalar.activation(qz[s][hd, h, 0:SEQ], bank[0][hd, :], ACT.Copy, scale=SCALE)
                ins.then_inc(q_ev, 1)

            def small_copy(n, s):
                act.wait_ge(small_mm, n + 1)
                for h in range(2):
                    hd = slice(h * HD, (h + 1) * HD)
                    nc.scalar.activation(qz[s][hd, h, SEQ:TOKENS], bank[2][hd, 0:DEC], ACT.Copy, scale=SCALE)
                nc.scalar.copy(kt[s][:, SEQ + KEEP:KCOLS], bank[2][:, DEC:2 * DEC])
                nc.scalar.copy(kt[s][:, SEQ:SEQ + KEEP], bank[2][:, P:2 * P]).then_inc(small_ev, 1)

            def key_row_copy(n, s, k):
                act.wait_ge(krow_mm, n + 1)
                act.wait_ge(kv_out[s], 64 * k + 16)
                nc.scalar.copy(k_rows[:, s, 0, :], bank[2][:, 0:P])
                nc.scalar.copy(k_rows[0:DEC, s, 1, :], bank[2][0:DEC, P:2 * P]).then_inc(krow_ev, 1)

            def exps(n, uu):
                h, i, q, nk = unit(uu)
                act.wait_ge(maxed, n * UNITS + uu + 1)
                b = uu % 5
                nc.scalar.activation(prob[0:q, b, 0:nk], prob[0:q, b, 0:nk], ACT.Exp, bias=soft[0:q, 0, b:b + 1],
                                     accum_out=soft[0:q, 1, b:b + 1]).then_inc(exped, 1)

            def pt_copy(n, uu):
                h, i, q, nk = unit(uu)
                act.wait_ge(pt_mm, n * UNITS + uu + 1)
                b = uu % 2
                if i is None:
                    nc.scalar.copy(pt[:, b, 0:DEC], bank[5 + b][:, 0:DEC])
                    nc.scalar.copy(pt[0:DEC, b, DEC:2 * DEC], bank[5 + b][0:DEC, DEC:2 * DEC]).then_inc(pt_ev, 1)
                else:
                    nc.scalar.copy(pt[:, b, 0:nk], bank[5 + b][:, 0:nk]).then_inc(pt_ev, 1)

            def pair(n, s, k, more):
                s2 = (s + 1) % 2
                exps(n, 0)
                exps(n, 1)
                if more:
                    query_copy(n + 1, s2)
                for uu in range(UNITS):
                    pt_copy(n, uu)
                    if uu + 2 < UNITS:
                        exps(n, uu + 2)
                    if uu == 5:
                        key_row_copy(n, s, k)
                    if uu == 7 and more:
                        small_copy(n + 1, s2)

            act.sem_inc(pt_ev, PT_LEAD)
            act.sem_inc(last_done, FREE)
            for m in (base, *extras):
                act.sem_inc(m.xt_ev_a, FREE)
                act.sem_inc(m.y_ev_a, FREE)
            act.wait_ge(consts, CONSTS)
            query_copy(0, 0)
            small_copy(0, 0)
            with act.Fori(0, PAIRS // 2 - 1) as it:
                for s in range(2):
                    pair(2 * it + s, s, it, True)
            for s in range(2):
                pair(PAIRS - 2 + s, s, PAIRS // 2 - 1, s == 0)

        def attn_dve(dve, steps):
            def key_copy(n, s):
                dve.wait_ge(k_mm, n + 1)
                nc.vector.tensor_copy(kt[s][:, 0:SEQ], bank[1][:]).then_inc(k_ev, 1)

            def value_copy(n, s, k):
                dve.wait_ge(v_mm, n + 1)
                dve.wait_ge(kv_out[s], 64 * k + 16)
                nc.vector.tensor_copy(vv[s][:, 0:TILES - 1, :], bank[0][:].rearrange("p (j n) -> p j n", n=P)).then_inc(v_ev, 1)

            def value4_copy(n, s, k):
                dve.wait_ge(v4_mm, n + 1)
                dve.wait_ge(kv_out[s], 64 * k + 16)
                nc.vector.tensor_copy(vv[s][0:DEC, TILES - 1, :], bank[1][0:DEC, 0:P]).then_inc(v4_ev, 1)

            def add_bias(n, uu):
                h, i, q, nk = unit(uu)
                g = n * UNITS + uu
                b, src = uu % 5, bank[3 + uu % 2]
                dve.wait_ge(score_mm, g + 1)
                dve.wait_ge(pt_ev, g - 4 + PT_LEAD)
                hh = 2 * n + h
                if i is None:
                    near, b0, far = nk, 0, 0
                else:
                    near = min(nk, WIN)
                    b0, far = WIN - near, nk - near
                if far:
                    nc.vector.tensor_scalar(prob[0:q, b, 0:far], src[0:q, 0:far], bias_flat[0:q, dyn(hh * WIN, 1)], None, ALU.add)
                nc.vector.tensor_tensor(prob[0:q, b, far:nk], src[0:q, far:nk],
                                        bias_flat[0:q, dyn(hh * WIN + b0, near)], ALU.add).then_inc(score_free, 1)
                dve.wait_ge(score_free, g + 1 + SC_LEAD)
                nc.vector.tensor_reduce(soft[0:q, 0, b:b + 1], prob[0:q, b, 0:nk], AX.X, ALU.max,
                                        negate=True).then_inc(maxed, 1)

            def normalise(n, uu):
                h, i, q, nk = unit(uu)
                b = uu % 5
                dve.wait_ge(exped, n * UNITS + uu + 1)
                steps.done(nc.vector.reciprocal(soft[0:q, 2, b:b + 1], soft[0:q, 1, b:b + 1]))
                nc.vector.tensor_scalar(prob[0:q, b, 0:nk], prob[0:q, b, 0:nk], soft[0:q, 2, b:b + 1], None,
                                        ALU.mult).then_inc(probs, 1)

            def sample_copy(n):
                dve.wait_ge(os_mm, n + 1)
                nc.vector.tensor_copy(xn_flat[:, dyn(n * TOKENS + SEQ, DEC)], bank[2][:, 0:DEC]).then_inc(os_ev, 1)

            def prompt_copy(n):
                dve.wait_ge(op_mm, n + 1)
                nc.vector.tensor_copy(xn_flat[:, dyn(n * TOKENS, SEQ)], bank[7][:]).then_inc(op_ev, 1)

            def pair(n, s, k, more):
                s2, k2 = (s + 1) % 2, k + (s + 1) // 2
                add_bias(n, 0)
                add_bias(n, 1)
                for uu in range(UNITS):
                    normalise(n, uu)
                    if uu + 2 < UNITS:
                        add_bias(n, uu + 2)
                    if uu == 3:
                        sample_copy(n)
                        if more:
                            key_copy(n + 1, s2)
                    if uu == 9 and more:
                        value_copy(n + 1, s2, k2)
                        value4_copy(n + 1, s2, k2)
                prompt_copy(n)

            dve.sem_inc(score_free, SC_LEAD)
            for begins_free in (op_ev, *(x for m in (base, *extras) for x in (m.xt_ev_d, m.y_ev_d, m.hid))):
                dve.sem_inc(begins_free, FREE)
            dve.wait_ge(bias_in, 16)
            nc.vector.memset(bias[0:CHUNK, :, WIN - CHUNK:WIN], -BIG).then_inc(bias_masked, 1)
            dve.wait_ge(bias_masked, 1)
            key_copy(0, 0)
            value_copy(0, 0, 0)
            value4_copy(0, 0, 0)
            PER = 2 * UNITS
            with dve.Fori(0, PAIRS // 2 - 1) as it:
                steps.enter(it, PER)
                for s in range(2):
                    pair(2 * it + s, s, it, True)
            steps.leave(PAIRS // 2 - 1, PER)
            for s in range(2):
                pair(PAIRS - 2 + s, s, PAIRS // 2 - 1, s == 0)

        def cols(n):
            return dyn(n * P, P)

        def heads2d(a):
            return a.rearrange("t h d -> t (h d)")

        def attn_sync(sp):
            wq = w_qkv[0].rearrange("(p c) n -> p c n", c=C)

            def load(n, s):
                for w in range(3):
                    sp.dma_start(wa[s][:, w, :, :], wq[:, :, dyn(w * D + n * P, P)]).then_inc(wa_in[s], 16)
                sp.dma_start(kcache[:, s, :], heads2d(cache_attn_k[0, 0])[:, cols(n)]).then_inc(wa_in[s], 16)

            def load_v(n, s):
                sp.dma_start(vv[s][:, TILES, :], heads2d(cache_attn_v[0, 0])[:, cols(n)]).then_inc(vc_in[s], 16)

            sp.dma_start(rel_sb[0:HEADS, P - 1:P - 1 + WIN], rel_rev[0, :, 0:WIN]).then_inc(rel_in, 16)
            load(0, 0)
            load_v(0, 0)
            sp.wait_ge(rel_ext, 1)
            sp.dma_start(bias_rows.rearrange("r h m -> h r m"),
                         rel_sb[0:HEADS, 0:EXT].unsqueeze(1).to_broadcast([HEADS, P, EXT])).then_inc(rel_out, 16)
            load(1, 1)
            load_v(1, 1)
            sp.wait_ge(rel_out, 16)
            sp.dma_start(bias, bass.AP(bias_rows.tensor, P - 1, [[HEADS * EXT - 1, P], [EXT, HEADS], [1, WIN]])).then_inc(bias_in, 16)
            sp.dma_start(wo_sb, w_o[0].rearrange("(c p) n -> p c n", p=P)).then_inc(wo_in, 16)
            with sp.Fori(0, PAIRS // 2 - 1) as it:
                for s in range(2):
                    n = 2 * it + s
                    sp.wait_ge(v4_mm, n + 1)
                    load(n + 2, s)
                    sp.wait_ge(os_mm, n + 1)
                    load_v(n + 2, s)
            sp.wait_ge(consts, CONSTS)
            for s, (a, b) in enumerate(((0, OPAIRS // 2), (OPAIRS // 2, OPAIRS))):
                sp.dma_start(y_sorted[EXPERTS * CAP + a * P:EXPERTS * CAP + b * P, :].rearrange("(a p) d -> p a d", p=P),
                             gain[:, 1, :].unsqueeze(1).to_broadcast([P, b - a, D])).then_inc(base.y_out[s], 16)

        def attn_pool(pool):
            def store(n, s):
                pool.wait_ge(krow_ev, n + 1)
                pool.wait_ge(v_ev, n + 1)
                pool.wait_ge(v4_ev, n + 1)
                for src, dst in ((k_rows[:, s, 0, :], kp_out[0, 0]), (vv[s][:, TILES - 2, :], vp_out[0, 0])):
                    pool.dma_start(heads2d(dst)[:, cols(n)], src).then_inc(kv_out[s], 16)
                for src, dst in ((k_rows[0:DEC, s, 1, :], ks_out[0, 0]), (vv[s][0:DEC, TILES - 1, :], vs_out[0, 0])):
                    pool.dma_start(heads2d(dst)[KEEP - DEC:KEEP, cols(n)], src).then_inc(kv_out[s], 16)

            zeros = lambda a: gain[:, 1, :].unsqueeze(1).to_broadcast([P, a, D])
            x_rows = x_sorted.rearrange("(a p) d -> p a d", p=P)
            few = SLOTS // P // PAIRS
            with pool.Fori(0, PAIRS // 2) as it:
                for s in range(2):
                    store(2 * it + s, s)
                    pool.dma_start(x_rows[:, dyn((2 * it + s) * few, few), :], zeros(few)).then_inc(zeros_in, 16)
            rest = SLOTS // P - PAIRS * few
            pool.dma_start(x_rows[:, PAIRS * few:SLOTS // P, :], zeros(rest)).then_inc(zeros_in, 16)

        RANKS, COUNTS = TILES * EXPERTS, slice(TILES * EXPERTS, (TILES + 1) * EXPERTS)

        def logits_pe(pe, l, j):
            pe.wait_ge(turn_ev_a, TILES * (2 * l + 1) + j + 1)
            pe.wait_ge(turn_ev_d, TILES * (2 * l + 1) + j + 1)
            if j == 0:
                pe.wait_ge(small_in, 64 * (l + 1))
            if TILES * l + j >= 1:
                pe.wait_ge(picks, TILES * l + j)
            for c in range(C):
                mm = nc.tensor.matmul(bank[5][0:rows[j], 0:RC], xw[:, c, j * P:j * P + rows[j]], router_w[:, c, :],
                                      start=c == 0, stop=c == C - 1)
            mm.then_inc(route_mm, 1)

        def ranks_pe(pe, l, j):
            pe.wait_ge(picks, TILES * l + j + 1)
            out = bank[6][:, j * EXPERTS:(j + 1) * EXPERTS]
            mm = nc.tensor.matmul(out, lower[:], picked[:, j, :], start=True, stop=j == 0)
            for b in range(j):
                mm = nc.tensor.matmul(out, ones[:], picked[:, b, :], start=False, stop=b == j - 1)
            if j == TILES - 1:
                for b in range(TILES):
                    mm = nc.tensor.matmul(bank[6][:, COUNTS], ones[:], picked[:, b, :], start=b == 0, stop=b == TILES - 1)
                mm.then_inc(ranks, 1)

        def router_act(act, l):
            act.wait_ge(gates_max, l + 1)
            nc.scalar.activation(gexp[:], gexp[:], ACT.Exp).then_inc(gates_exp, 1)
            act.wait_ge(second, l + 1)
            nc.scalar.activation(tok[:, 6, :], tok[:, 6, :], ACT.Exp).then_inc(second_exp, 1)

        def choose_dve(dve, steps, l, j):
            V, do, r = nc.vector, steps.done, rows[j]
            t = lambda i: tok[0:r, i, j:j + 1]
            lg, le = logits[0:r, j, 0:GROUPS], logits[0:r, j, GROUPS:RC]
            kept, second_of, some = held[0:r, 0, :], held[0:r, 1, :], cand[0:r, :]
            dve.wait_ge(route_mm, TILES * l + j + 1)
            do(V.tensor_tensor(logits[0:r, j, :], bank[5][0:r, 0:RC], router_b[0:r, :], ALU.add))
            do(V.tensor_reduce(t(0), lg, AX.X, ALU.max))
            few = down_iota[0:r, EXPERTS - GROUPS:EXPERTS]
            do(V.scalar_tensor_tensor(some[:, 0:GROUPS], lg, t(0), few, ALU.is_equal, ALU.mult))
            do(V.tensor_reduce(t(1), some[:, 0:GROUPS], AX.X, ALU.max))
            do(V.tensor_scalar(pen[0:r, :], few, t(1), -BIG, ALU.not_equal, ALU.mult))
            grouped = lambda a: a.rearrange("p (g e) -> p g e", g=GROUPS)
            do(V.tensor_tensor(grouped(kept), grouped(le), pen[0:r, :].unsqueeze(2).to_broadcast([r, GROUPS, PER_GROUP]),
                               ALU.add))
            do(V.tensor_reduce(t(2), kept, AX.X, ALU.max))
            do(V.scalar_tensor_tensor(some, kept, t(2), down_iota[0:r, :], ALU.is_equal, ALU.mult))
            do(V.tensor_reduce(t(3), some, AX.X, ALU.max))
            do(V.tensor_scalar(hot[0:r, 0, j, :], down_iota[0:r, :], t(3), None, ALU.is_equal))
            do(V.scalar_tensor_tensor(second_of, hot[0:r, 0, j, :], -BIG, kept, ALU.mult, ALU.add))
            do(V.tensor_reduce(t(4), second_of, AX.X, ALU.max))
            do(V.scalar_tensor_tensor(some, second_of, t(4), down_iota[0:r, :], ALU.is_equal, ALU.mult))
            do(V.tensor_reduce(t(5), some, AX.X, ALU.max))
            V.scalar_tensor_tensor(picked[0:r, j, :], down_iota[0:r, :], t(5), hot[0:r, 0, j, :], ALU.is_equal,
                                   ALU.add).then_inc(picks, 1)
            do(V.tensor_scalar(hot[0:r, 1, j, :], down_iota[0:r, :], t(5), None, ALU.is_equal))

        def router_dve(dve, steps, l):
            V, do = nc.vector, steps.done

            def over_tiles(a):
                return a.unsqueeze(1).to_broadcast([P, TILES, EXPERTS])

            rank = bank[6][:, 0:RANKS].rearrange("p (j e) -> p j e", e=EXPERTS)
            dve.wait_ge(ranks, l + 1)
            do(V.tensor_tensor(qcmp[:], bank[6][:, COUNTS].unsqueeze(2).to_broadcast([P, EXPERTS, MAXQ]),
                               qrow[:].unsqueeze(1).to_broadcast([P, EXPERTS, MAXQ]), ALU.is_gt))
            do(V.tensor_reduce(more_tiles[:], qcmp[:], AX.X, ALU.add))
            do(V.tensor_tensor_scan(ends[:, 1:1 + EXPERTS], more_tiles[:], zero_e[:], 0.0, ALU.add, ALU.add))
            do(V.scalar_tensor_tensor(shift[:], ends[:, 0:EXPERTS], float(CAP), more_row[:], ALU.mult, ALU.add))
            do(V.tensor_tensor(place[:, 0, :, :], rank, over_tiles(first_row[:]), ALU.add))
            do(V.scalar_tensor_tensor(place[:, 1, :, :], rank, float(CAP), over_tiles(shift[:]), ALU.is_ge, ALU.mult))
            do(V.tensor_tensor(place[:, 0, :, :], place[:, 0, :, :], place[:, 1, :, :], ALU.add))
            do(V.tensor_tensor(at_slot[:], hot[:], place[:, 0, :, :].unsqueeze(1).to_broadcast([P, 2, TILES, EXPERTS]),
                               ALU.mult))
            do(V.tensor_reduce(slot_f[:], at_slot[:], AX.X, ALU.add))
            V.tensor_copy(slot[:], slot_f[:]).then_inc(routed, 1)
            do(V.tensor_tensor(ocmp[:], orow[:].unsqueeze(2).to_broadcast([P, OVER, EXPERTS]),
                               ends[:, 1:1 + EXPERTS].unsqueeze(1).to_broadcast([P, OVER, EXPERTS]), ALU.is_ge))
            do(V.tensor_reduce(oexp[:], ocmp[:], AX.X, ALU.add))
            do(V.tensor_scalar(over_expert[:], oexp[:], float(EXPERTS - 1), None, ALU.min))
            do(V.tensor_scalar(ofew[:], orow[:, 0:OVER:2], ends[:, EXPERTS:EXPERTS + 1], None, ALU.is_lt))
            do(V.tensor_reduce(opairs[:], ofew[:], AX.X, ALU.add))
            do(V.tensor_copy(over_count[:], opairs[:]))
            dve.sem_inc(further_known, 1)
            V.tensor_tensor(gexp[:], logits[:, :, 0:GROUPS], tok[:, 0, :].unsqueeze(2).to_broadcast([P, TILES, GROUPS]),
                            ALU.subtract).then_inc(gates_max, 1)
            V.tensor_tensor(tok[:, 6, :], tok[:, 4, :], tok[:, 2, :], ALU.subtract).then_inc(second, 1)
            dve.wait_ge(gates_exp, l + 1)
            do(V.tensor_reduce(tok[:, 7, :], gexp[:], AX.X, ALU.add))
            dve.wait_ge(second_exp, l + 1)
            do(V.tensor_scalar(tok[:, 8, :], tok[:, 6, :], 1.0, None, ALU.add))
            do(V.tensor_tensor(tok[:, 8, :], tok[:, 8, :], tok[:, 7, :], ALU.mult))
            do(V.reciprocal(gate_w[:, 0, :], tok[:, 8, :]))
            do(V.tensor_tensor(gate_w[:, 1, :], gate_w[:, 0, :], tok[:, 6, :], ALU.mult))

        def scatter_pool(pool, l):
            pool.wait_ge(routed, l + 1)
            pool.wait_ge(normed, TILES * (2 * l + 2))
            if l == 0:
                pool.wait_ge(zeros_in, 16 * (PAIRS + 1))
            for j in range(TILES):
                for k in range(2):
                    pool.indirect_dma_start(x_sorted, bass.IndirectOffsetOnAxis(slot[0:rows[j], k, j:j + 1], 0),
                                            xf[0:rows[j], j, :], None, bounds_check=SLOTS - 1,
                                            oob_is_err=True).then_inc(scattered, 16)

        def gather_pool(pool, l):
            for s in range(2):
                pool.wait_ge(base.y_out[s], 16 * (EPAIRS // 2) * (l + 1) + 16)
            pool.wait_ge(extra_end, l + 1)
            for j in range(TILES):
                for k in range(2):
                    dst = (xn, yg)[k]
                    pool.indirect_dma_start(dst[0:rows[j], j, :], None, y_sorted,
                                            bass.IndirectOffsetOnAxis(slot[0:rows[j], k, j:j + 1], 0),
                                            bounds_check=SLOTS - 1, oob_is_err=True).then_inc(gathered[j], 16)

        def combine_dve(dve, steps, l, j):
            r = rows[j]
            dve.wait_ge(gathered[j], 32 * (l + 1))
            steps.done(nc.vector.scalar_tensor_tensor(x[0:r, j, :], xn[0:r, j, :], gate_w[0:r, 0, j:j + 1],
                                                      x[0:r, j, :], ALU.mult, ALU.add))
            nc.vector.scalar_tensor_tensor(x[0:r, j, :], yg[0:r, j, :], gate_w[0:r, 1, j:j + 1],
                                           x[0:r, j, :], ALU.mult, ALU.add).then_inc(combined, 1)

        def ex_turn_pe(pe, m, i, s, k):
            pe.wait_ge(m.x_in[s], 16 * (k + 1))
            pe.wait_ge(m.xt_ev_a, i + FREE)
            pe.wait_ge(m.xt_ev_d, i + FREE)
            for c in range(C):
                mm = nc.tensor.transpose(bank[c // 4][:, (c % 4) * P:(c % 4 + 1) * P], xe[s][:, c * P:(c + 1) * P], ident[:])
            mm.then_inc(m.xt_mm, 1)

        def ex_up_pe(pe, m, i, s, k, loads):
            pe.wait_ge(m.xt_ev_a, i + 1 + FREE)
            pe.wait_ge(m.xt_ev_d, i + 1 + FREE)
            pe.wait_ge(m.gu_in[s], 16 * loads * (k + 1))
            for c in range(C):
                for e in range(2):
                    rr = slice(CAP * e, CAP * (e + 1))
                    mm = nc.tensor.matmul(bank[2 + s][rr, :], xte[s][:, c, rr], wgu[s][:, :, e, c, :],
                                          start=c == 0, stop=c == C - 1)
            mm.then_inc(m.gu_mm, 1)

        def ex_down_pe(pe, m, i, s, k, loads):
            pe.wait_ge(m.hid, i + 1 + FREE)
            for c in range(FC):
                mm = nc.tensor.transpose(bank[4][:, c * P:(c + 1) * P], hid[:, c * P:(c + 1) * P], ident[:])
            mm.then_inc(m.ht_mm, 1)
            pe.wait_ge(m.ht_ev, i + 1)
            pe.wait_ge(m.dn_in[s], 16 * loads * (k + 1))
            pe.wait_ge(m.y_ev_a, i + FREE)
            pe.wait_ge(m.y_ev_d, i + FREE)
            for h in range(2):
                for c in range(FC):
                    for e in range(2):
                        rr = slice(CAP * e, CAP * (e + 1))
                        mm = nc.tensor.matmul(bank[5 + h][rr, :], hts[:, c, rr], wdn[s][:, e, c, h * HALF:(h + 1) * HALF],
                                              start=c == 0, stop=c == FC - 1)
            mm.then_inc(m.dn_mm, 1)

        def ex_turn_copy(eng, copy, m, i, s, half, done):
            eng.wait_ge(m.xt_mm, i + 1)
            copy(xte[s][:, 4 * half:4 * half + 4, :], bank[half][:].rearrange("p (c r) -> p c r", c=4)).then_inc(done, 1)

        def ex_silu_act(act, m, i, s):
            act.wait_ge(m.gu_mm, i + 1)
            act.wait_ge(m.hid, i + FREE)
            nc.scalar.activation(sg, bank[2 + s][:, 0:FE], ACT.Silu).then_inc(m.silu, 1)

        def ex_hid_dve(dve, m, i, s):
            dve.wait_ge(m.silu, i + 1)
            nc.vector.tensor_tensor(hid_cp, sg.rearrange("p (q c) -> p q c", c=FC),
                                    bank[2 + s][:, FE:2 * FE].rearrange("p (q c) -> p q c", c=FC), ALU.mult).then_inc(m.hid, 1)

        def ex_ht_dve(dve, m, i):
            dve.wait_ge(m.ht_mm, i + 1)
            nc.vector.tensor_copy(hts, bank[4][:, 0:FE].rearrange("p (c r) -> p c r", c=FC)).then_inc(m.ht_ev, 1)

        def ex_y_copy(eng, copy, m, i, s, k, half, done):
            eng.wait_ge(m.dn_mm, i + 1)
            if m is base:
                eng.wait_ge(m.y_out[s], 16 * k + 16)
            else:
                eng.wait_ge(m.y_free, i + FREE)
            copy(ysb[s][:, half * HALF:(half + 1) * HALF], bank[5 + half][:]).then_inc(done, 1)

        def rows_of(a, i):
            return a[dyn(i * P, P), :]

        def turns(eng, body, l):
            first = EPAIRS * l
            with eng.Fori(0, EPAIRS // 2 - 1) as it:
                for s in range(2):
                    body(first + 2 * it + s, s, first // 2 + it, 2 * it + s, True)
            for s in range(2):
                body(first + EPAIRS - 2 + s, s, (first + EPAIRS) // 2 - 1, EPAIRS - 2 + s, s == 0)

        def extra_turns(eng, l, body):
            eng.wait_ge(further_known, l + 1)
            count = eng.value_load(over_count[0:1, 0:1], min_val=0, max_val=OPAIRS)
            with eng.If(count > 0):
                with eng.Fori(0, count) as it:
                    body(it)

        def experts_pe(pe, l):
            ex_turn_pe(pe, base, EPAIRS * l, 0, EPAIRS // 2 * l)

            def body(i, s, k, local, more):
                ex_up_pe(pe, base, i, s, k, 2)
                if more:
                    ex_turn_pe(pe, base, i + 1, (s + 1) % 2, k + (s + 1) // 2)
                ex_down_pe(pe, base, i, s, k, 1)

            turns(pe, body, l)

            extra = extras[l]

            def further(i):
                ex_turn_pe(pe, extra, i, 0, i)
                ex_up_pe(pe, extra, i, 0, i, 4)
                ex_down_pe(pe, extra, i, 0, i, 2)

            extra_turns(pe, l, further)

        def experts_act(act, l):
            ex_turn_copy(act, nc.scalar.copy, base, EPAIRS * l, 0, 0, base.xt_ev_a)

            def body(i, s, k, local, more):
                ex_silu_act(act, base, i, s)
                if more:
                    ex_turn_copy(act, nc.scalar.copy, base, i + 1, (s + 1) % 2, 0, base.xt_ev_a)
                ex_y_copy(act, nc.scalar.copy, base, i, s, k, 0, base.y_ev_a)

            turns(act, body, l)

            extra = extras[l]

            def further(i):
                ex_turn_copy(act, nc.scalar.copy, extra, i, 0, 0, extra.xt_ev_a)
                ex_silu_act(act, extra, i, 0)
                ex_y_copy(act, nc.scalar.copy, extra, i, 0, i, 0, extra.y_ev_a)

            extra_turns(act, l, further)

        def experts_dve(dve, l):
            ex_turn_copy(dve, nc.vector.tensor_copy, base, EPAIRS * l, 0, 1, base.xt_ev_d)

            def body(i, s, k, local, more):
                ex_hid_dve(dve, base, i, s)
                if more:
                    ex_turn_copy(dve, nc.vector.tensor_copy, base, i + 1, (s + 1) % 2, 1, base.xt_ev_d)
                ex_ht_dve(dve, base, i)
                ex_y_copy(dve, nc.vector.tensor_copy, base, i, s, k, 1, base.y_ev_d)

            turns(dve, body, l)

            extra = extras[l]

            def further(i):
                ex_turn_copy(dve, nc.vector.tensor_copy, extra, i, 0, 1, extra.xt_ev_d)
                ex_hid_dve(dve, extra, i, 0)
                ex_ht_dve(dve, extra, i)
                ex_y_copy(dve, nc.vector.tensor_copy, extra, i, 0, i, 1, extra.y_ev_d)

            extra_turns(dve, l, further)

        def gu_load(sp, l, p, s):
            for w, src in enumerate((w_gate, w_up)):
                sp.dma_start(wgu[s][:, w, :, :, :].rearrange("p e c f -> p e (c f)"),
                             src[l, dyn(2 * p, 2)].rearrange("e (p c) f -> p e (c f)", c=C)).then_inc(base.gu_in[s], 16)

        def dn_load(sp, l, p, s):
            sp.dma_start(wdn[s].rearrange("p e c n -> p e (c n)"),
                         w_down[l, dyn(2 * p, 2)].rearrange("e (p c) n -> p e (c n)", c=FC)).then_inc(base.dn_in[s], 16)

        def first_loads(sp, l, s):
            if s == 0 and l == 0:
                sp.wait_ge(op_ev, PAIRS + FREE)
                for b in range(2):
                    sp.wait_ge(kv_out[b], 64 * PAIRS // 2 + 16)
            if s == 1 and l == 0:
                dn_load(sp, l, s, s)
            if s == 1:
                sp.wait_ge(proj_mm, 2 * TILES * (l + 1))
            if s == 1 and l == 1:
                sp.wait_ge(proj_ev, 2 * TILES * (l + 1))
            gu_load(sp, l, s, s)
            if s == 0 or l == 1:
                dn_load(sp, l, s, s)

        def experts_sync(sp, l):
            sp.wait_ge(scattered, 16 * 2 * TILES * (l + 1))
            for s in range(2):
                sp.dma_start(xe[s], rows_of(x_sorted, s)).then_inc(base.x_in[s], 16)

            def body(i, s, local, more):
                if more:
                    sp.wait_ge(base.xt_mm, i + 1)
                    sp.dma_start(xe[s], rows_of(x_sorted, local + 2)).then_inc(base.x_in[s], 16)
                    sp.wait_ge(base.gu_mm, i + 1)
                    gu_load(sp, l, local + 2, s)
                    sp.wait_ge(base.dn_mm, i + 1)
                    dn_load(sp, l, local + 2, s)
                sp.wait_ge(base.y_ev_a, i + 1 + FREE)
                sp.wait_ge(base.y_ev_d, i + 1 + FREE)
                sp.dma_start(rows_of(y_sorted, local), ysb[s]).then_inc(base.y_out[s], 16)

            extra = extras[l]

            def extra_loads(o):
                sp.dma_start(xe[0], rows_of(x_sorted, EPAIRS + o)).then_inc(extra.x_in[0], 16)
                for e in range(2):
                    expert = sp.value_load(over_expert[0:1, dyn(2 * o + e, 1)], min_val=0, max_val=EXPERTS - 1)
                    for w, src in enumerate((w_gate, w_up)):
                        sp.dma_start(wgu[0][:, w, e, :, :].rearrange("p c f -> p (c f)"),
                                     src[l, dyn(expert, 1)].rearrange("e (p c) f -> p (e c f)", c=C)).then_inc(extra.gu_in[0], 16)
                    sp.dma_start(wdn[0][:, e, :, :].rearrange("p c n -> p (c n)"),
                                 w_down[l, dyn(expert, 1)].rearrange("e (p c) n -> p (e c n)", c=FC)).then_inc(extra.dn_in[0], 16)

            def extra_store(o):
                sp.wait_ge(extra.y_ev_a, o + 1 + FREE)
                sp.wait_ge(extra.y_ev_d, o + 1 + FREE)
                sp.dma_start(rows_of(y_sorted, EPAIRS + o), ysb[0]).then_inc(extra.y_out[0], 16)
                sp.wait_ge(extra.y_out[0], 16 * (o + 1))
                sp.sem_inc(extra.y_free, 1)

            sp.sem_inc(extra.y_free, FREE)
            sp.wait_ge(further_known, l + 1)
            count = sp.value_load(over_count[0:1, 0:1], min_val=0, max_val=OPAIRS)
            with sp.Fori(0, EPAIRS // 2 - 1) as it:
                for s in range(2):
                    body(EPAIRS * l + 2 * it + s, s, 2 * it + s, True)
            body(EPAIRS * (l + 1) - 2, 0, EPAIRS - 2, False)
            with sp.If(count > 0):
                extra_loads(0)
            body(EPAIRS * (l + 1) - 1, 1, EPAIRS - 1, False)
            for s in range(2):
                sp.wait_ge(base.y_out[s], 16 * (EPAIRS // 2) * (l + 1) + 16)
            with sp.If(count > 1):
                with sp.Fori(1, count) as o:
                    extra_store(o - 1)
                    extra_loads(o)
            with sp.If(count > 0):
                extra_store(count - 1)
            sp.sem_inc(extra_end, 1)

        def conv_load(sp, cc, s):
            wp1 = w_pw1[0].rearrange("(p c) n -> p c n", c=C)

            for w in range(2):
                sp.dma_start(wp[s][:, w, :, :], wp1[:, :, dyn(w * D + cc * P, P)]).then_inc(wp_in[s], 16)

        def conv_first(sp):
            sp.dma_start(raw[0:TAPS, :], w_dw[0]).then_inc(raw_in, 16)
            for n, row in enumerate((b_dw[0], ln_g[0], ln_b[0], b_pw1[0, 0:D], b_pw1[0, D:2 * D])):
                sp.dma_start(raw[TAPS + n:TAPS + n + 1, :], row.rearrange("(a n) -> a n", a=1)).then_inc(raw_in, 16)
            sp.wait_ge(gathered[TILES - 2], 32)
            for s in range(2):
                conv_load(sp, s, s)

        def conv_sync(sp):
            sp.wait_ge(combined, TILES)
            sp.dma_start(w2, w_pw2[0].rearrange("(c p) n -> p c n", p=P)).then_inc(w2_in, 16)
            first_loads(sp, 1, 0)
            with sp.Fori(0, C // 2 - 1) as it:
                for s in range(2):
                    sp.wait_ge(glu_mm, 2 * it + s + 1)
                    conv_load(sp, 2 * it + s + 2, s)

        def conv_small_pe(pe):
            pe.wait_ge(raw_in, 16 * 6)
            for c in range(C):
                mm = nc.tensor.transpose(bank[5][:, c * NV:(c + 1) * NV], raw[0:NV, c * P:(c + 1) * P], ident[0:NV, 0:NV])
            mm.then_inc(raw_mm, 1)
            pe.wait_ge(cache_in, 16)
            for c in range(C):
                mm = nc.tensor.transpose(bank[6][:, c * STATE:(c + 1) * STATE], conv_cache[0:STATE, c * P:(c + 1) * P],
                                         ident[0:STATE, 0:STATE])
            mm.then_inc(raw_mm, 1)

        def conv_pe(pe):
            conv_small_pe(pe)
            pe.wait_ge(turn_ev_a, TILES * 3)
            pe.wait_ge(turn_ev_d, TILES * 3)

            def glu(n, s, k):
                pe.wait_ge(wp_in[s], 32 * (k + 1))
                pe.wait_ge(glu_done, n - 1 + CONV_LEAD)
                for w in range(2):
                    for c in range(C):
                        nc.tensor.matmul(bank[3 * s + w][:], wp[s][:, w, c, :], xt[:, c, 0:SEQ], start=c == 0, stop=c == C - 1)
                for w in range(2):
                    for c in range(C):
                        mm = nc.tensor.matmul(bank[3 * s + 2][:, w * DEC:(w + 1) * DEC], wp[s][:, w, c, :],
                                              xt[:, c, SEQ:TOKENS], start=c == 0, stop=c == C - 1)
                mm.then_inc(glu_mm, 1)

            def taps(n, s):
                pe.wait_ge(glu_done, n + 1 + CONV_LEAD)
                pe.wait_ge(diag_done, n + 1)
                pe.wait_ge(conv_done, n + CONV_LEAD)
                for b, at, m in ((6, 0, SEQ), (7, STATE + SEQ, DEC)):
                    for t in range(PE_TAPS):
                        mm = nc.tensor.matmul(bank[b][:, 0:m], diag[s][:, t, :], u[s][:, at + t:at + t + m],
                                              start=t == 0, stop=t == PE_TAPS - 1)
                mm.then_inc(conv_mm, 1)

            pe.wait_ge(raw_ev, 2)
            glu(0, 0, 0)
            with pe.Fori(0, C // 2 - 1) as it:
                for s in range(2):
                    glu(2 * it + s + 1, 1 - s, it + s)
                    taps(2 * it + s, s)
            glu(C - 1, 1, C // 2 - 1)
            for s in range(2):
                taps(C - 2 + s, s)
            pe.wait_ge(glu_done, C + CONV_LEAD)
            for c in range(C):
                pe.wait_ge(conv_done, c + 1 + CONV_LEAD)
                nc.tensor.matmul(bank[5][:], mean_w[:], dw[:, c, 0:SEQ], start=c == 0, stop=c == C - 1)
                mm = nc.tensor.matmul(bank[4][:, 0:DEC], mean_w[:], dw[:, c, SEQ:TOKENS], start=c == 0, stop=c == C - 1)
            mm.then_inc(mean_mm, 1)
            pe.wait_ge(last_done, C + FREE)
            for c in range(C):
                mm = nc.tensor.transpose(bank[c // 4][0:2 * STATE, (c % 4) * P:(c % 4 + 1) * P], last_u[:, c, :], ident[:])
            mm.then_inc(last_mm, 1)
            for c in range(C):
                pe.wait_ge(sq_done, c + 1)
                nc.tensor.matmul(bank[6][:], mean_w[:], sq[:, c, 0:SEQ], start=c == 0, stop=c == C - 1)
                mm = nc.tensor.matmul(bank[7][:, 0:DEC], mean_w[:], sq[:, c, SEQ:TOKENS], start=c == 0, stop=c == C - 1)
            mm.then_inc(var_mm, 1)
            pe.wait_ge(w2_in, 16)
            project_pe(pe, 1, dw, w2, swished)

        def conv_act(act, steps):
            act.wait_ge(raw_mm, 1)
            nc.scalar.copy(chan, bank[5][:, 0:C * NV].rearrange("p (c v) -> p c v", c=C)).then_inc(raw_ev, 1)
            act.wait_ge(raw_mm, 2)
            nc.scalar.copy(state, bank[6][:, 0:C * STATE].rearrange("p (c k) -> p c k", c=C)).then_inc(raw_ev, 1)
            act.wait_ge(raw_ev, 2)

            def fill(n, s):
                act.wait_ge(conv_done, n - 1 + CONV_LEAD)
                nc.scalar.copy(cvec[s], chan_flat[:, dyn(n * NV, NV)])
                nc.scalar.copy(u[s][:, STATE + SEQ:2 * STATE + SEQ],
                               state_flat[:, dyn(n * STATE, STATE)]).then_inc(u_filled, 1)

            def chunk(n, s):
                fill(n, s)
                act.wait_ge(u_filled, n + 1)
                for t in range(PE_TAPS):
                    ins = nc.scalar.activation(diag[s][:, t, :], ident[:], ACT.Copy, scale=cvec[s][:, t:t + 1])
                ins.then_inc(diag_done, 1)
                act.wait_ge(glu_mm, n + 1)
                act.wait_ge(glu_done, n + CONV_LEAD)
                g = cvec[s][:, TAPS + 4:TAPS + 5]
                nc.scalar.activation(sig[:, 0:SEQ], bank[3 * s + 1][:], ACT.Sigmoid, bias=g)
                nc.scalar.activation(sig[:, SEQ:TOKENS], bank[3 * s + 2][:, DEC:2 * DEC], ACT.Sigmoid, bias=g).then_inc(sig_done, 1)
                act.wait_ge(glu_done, n + 1 + CONV_LEAD)
                nc.scalar.copy(last_flat[:, dyn(2 * n * STATE, STATE)], u[s][:, SEQ:SEQ + STATE])
                nc.scalar.copy(last_flat[:, dyn((2 * n + 1) * STATE, STATE)], u[s][:, SPAN - STATE:SPAN]).then_inc(last_done, 1)

            with act.Fori(0, C // 2) as it:
                for s in range(2):
                    chunk(2 * it + s, s)
            act.wait_ge(last_mm, 1)
            for h in range(2):
                ins = nc.scalar.copy(last_rows[0:2 * STATE, h * HALF:(h + 1) * HALF], bank[h][0:2 * STATE, :])
            ins.then_inc(last_ev, 1)
            for c in range(C):
                act.wait_ge(centred, c + 1)
                nc.scalar.activation(sq[:, c, :], dw[:, c, :], ACT.Square).then_inc(sq_done, 1)
            act.wait_ge(var_mm, 1)
            nc.scalar.activation(sig[:, 0:SEQ], bank[6][:], ACT.Sqrt, bias=ln_eps[:])
            nc.scalar.activation(sig[:, SEQ:TOKENS], bank[7][:, 0:DEC], ACT.Sqrt, bias=ln_eps[:]).then_inc(std_done, 1)
            for c in range(C):
                act.wait_ge(scaled, c + 1)
                nc.scalar.activation(dw[:, c, :], dw[:, c, :], ACT.Silu, bias=chan[:, c, TAPS + 2:TAPS + 3],
                                     scale=chan[:, c, TAPS + 1:TAPS + 2]).then_inc(swished, 1)

        CONV_LEAD = 2
        conv_cache = sb("conv_cache", [STATE, D])
        last_rows = raw

        def conv_dve(dve, steps):
            V = nc.vector
            dve.sem_inc(conv_done, CONV_LEAD)
            dve.sem_inc(glu_done, CONV_LEAD)
            for s in range(2):
                steps.done(V.memset(u[s][:, 0:STATE], 0.0))

            def gated(n, s):
                a = cvec[s][:, TAPS + 3:TAPS + 4]
                dve.wait_ge(u_filled, n + 1)
                dve.wait_ge(sig_done, n + 1)
                V.scalar_tensor_tensor(u[s][:, STATE:STATE + SEQ], bank[3 * s][:], a, sig[:, 0:SEQ], ALU.add, ALU.mult)
                V.scalar_tensor_tensor(u[s][:, SPAN - DEC:SPAN], bank[3 * s + 2][:, 0:DEC], a, sig[:, SEQ:TOKENS],
                                       ALU.add, ALU.mult).then_inc(glu_done, 1)
                dve.wait_ge(glu_done, n + 1 + CONV_LEAD)

            def taps(n, s):
                w = lambda t: cvec[s][:, t:t + 1]
                t = PE_TAPS
                steps.done(V.tensor_scalar(acc[s], u[s][:, t:t + OUTS], w(t), cvec[s][:, TAPS:TAPS + 1], ALU.mult, ALU.add))
                for t in range(PE_TAPS + 1, TAPS):
                    steps.done(V.scalar_tensor_tensor(acc[s], u[s][:, t:t + OUTS], w(t), acc[s], ALU.mult, ALU.add))

            def add(n, s):
                dve.wait_ge(conv_mm, n + 1)
                dve.wait_ge(last_done, n + FREE)
                V.tensor_tensor(xn_flat[:, dyn(n * TOKENS, SEQ)], bank[6][:], acc[s][:, 0:SEQ], ALU.add)
                V.tensor_tensor(xn_flat[:, dyn(n * TOKENS + SEQ, DEC)], bank[7][:, 0:DEC], acc[s][:, OUTS - DEC:OUTS],
                                ALU.add).then_inc(conv_done, 1)

            dve.wait_ge(raw_ev, 2)
            gated(0, 0)
            PER = 2 * (TAPS - PE_TAPS)
            with dve.Fori(0, C // 2 - 1) as it:
                steps.enter(it, PER)
                for s in range(2):
                    taps(2 * it + s, s)
                    gated(2 * it + s + 1, 1 - s)
                    add(2 * it + s, s)
            steps.leave(C // 2 - 1, PER)
            taps(C - 2, 0)
            gated(C - 1, 1)
            add(C - 2, 0)
            taps(C - 1, 1)
            add(C - 1, 1)
            dve.wait_ge(mean_mm, 1)
            for c in range(C):
                V.tensor_tensor(dw[:, c, 0:SEQ], dw[:, c, 0:SEQ], bank[5][:], ALU.subtract)
                V.tensor_tensor(dw[:, c, SEQ:TOKENS], dw[:, c, SEQ:TOKENS], bank[4][:, 0:DEC], ALU.subtract).then_inc(centred, 1)
            dve.wait_ge(std_done, 1)
            steps.done(V.reciprocal(sig[:], sig[:]))
            for c in range(C):
                V.tensor_tensor(dw[:, c, :], dw[:, c, :], sig[:], ALU.mult).then_inc(scaled, 1)
            dve.wait_ge(b2_in, 16)
            project_dve(dve, steps, 1, b2)

        CONSTS = 5

        block = ctx.enter_context(nc.Block())

        @block.sync
        def _(sp):
            for j in range(TILES):
                src = x_prompt[0, j * P:(j + 1) * P, :] if j < TILES - 1 else x_sample[0]
                sp.dma_start(x[0:rows[j], j, :], src).then_inc(x_in[j], 16)
                if j == 0:
                    sp.dma_start(gain[:, 0, :], broadcast(norm_mix[0])).then_inc(gain_in, 16)
            attn_sync(sp)
            sp.dma_start(conv_cache[:], cache_conv[0, 0]).then_inc(cache_in, 16)
            for l in range(LAYERS):
                if l == 1:
                    conv_first(sp)
                sp.wait_ge(normed, TILES * (2 * l + 1))
                sp.dma_start(gain[:, 0, :], broadcast(norm_ffn[l])).then_inc(gain_in, 16)
                for src, dst in ((w_group[l], router_w[:, :, 0:GROUPS]), (w_router[l], router_w[:, :, GROUPS:RC])):
                    sp.dma_start(dst, src.rearrange("(p c) n -> p c n", c=C)).then_inc(small_in, 16)
                for src, dst in ((b_group[l], router_b[:, 0:GROUPS]), (b_router[l], router_b[:, GROUPS:RC])):
                    sp.dma_start(dst, broadcast(src)).then_inc(small_in, 16)
                if l == 1:
                    conv_sync(sp)
                    sp.wait_ge(conv_done, C + CONV_LEAD)
                    sp.dma_start(b2, broadcast(b_pw2[0])).then_inc(b2_in, 16)
                    sp.wait_ge(last_ev, 1)
                    sp.dma_start(cp_out[0, 0], last_rows[0:STATE, :]).then_inc(out_done, 16)
                    sp.dma_start(cs_out[0, 0], last_rows[STATE:2 * STATE, :]).then_inc(out_done, 16)
                    sp.wait_ge(out_done, 32)
                if l == 0:
                    first_loads(sp, l, 0)
                first_loads(sp, l, 1)
                experts_sync(sp, l)
                sp.dma_start(gain[:, 0, :], broadcast(norm_mix[l + 1] if l + 1 < LAYERS else norm_final)).then_inc(gain_in, 16)
            for j in range(TILES):
                sp.wait_ge(normed, TILES * 2 * LAYERS + j + 1)
                dst = y_prompt[0, j * P:(j + 1) * P, :] if j < TILES - 1 else y_sample[0]
                sp.dma_start(dst, xn[0:rows[j], j, :]).then_inc(out_done, 16)
            sp.wait_ge(out_done, 16 * (TILES + 2))

        @block.gpsimd
        def _(pool):
            steps = Steps(pool, pool_steps)
            for t, fill, cmp, pat, mult, b in ((ident, 1.0, ALU.not_equal, [[-1, P]], 1, 0),):
                steps.done(pool.memset(t[:], 0.0))
                pool.affine_select(out=t[:], in_=t[:], compare_op=cmp, fill=fill, base=b, pattern=pat,
                                   channel_multiplier=mult).then_inc(ident0, 1)
            steps.done(pool.memset(ones[:], 1.0))
            steps.done(pool.affine_select(out=lower[:], in_=ones[:], compare_op=ALU.is_gt, fill=0.0, base=0,
                                          pattern=[[1, P]], channel_multiplier=-1))
            steps.done(pool.memset(mean_w[:], 1.0 / D))
            steps.done(pool.memset(gain[:, 1, :], 0.0))
            for s in range(2):
                steps.done(pool.memset(qz[s][HD:P, 0, :], 0.0))
                steps.done(pool.memset(qz[s][0:HD, 1, :], 0.0))
            steps.done(pool.memset(logits[:], 0.0))
            steps.done(pool.memset(eps[:], 1e-6))
            steps.done(pool.memset(ln_eps[:], 1e-5))
            pool.sem_inc(consts, 1)
            steps.done(pool.iota(down_i[:], [[-1, EXPERTS]], base=EXPERTS, channel_multiplier=0))
            steps.done(pool.iota(up_i[:], [[1, OVER + EXPERTS]], base=0, channel_multiplier=0))
            steps.done(pool.tensor_copy(down_iota[:], down_i[:]))
            steps.done(pool.tensor_copy(orow[:], up_i[:, 0:OVER]))
            steps.done(pool.tensor_scalar(first_row[:], up_i[:, 0:EXPERTS], float(CAP), None, ALU.mult))
            steps.done(pool.tensor_scalar(more_row[:], down_iota[:], -1.0, float(CAP), ALU.add, ALU.mult))
            steps.done(pool.tensor_scalar(qrow[:], orow[:, 1:1 + MAXQ], float(CAP), None, ALU.mult))
            for t in (zero_e, hot, picked, tok):
                steps.done(pool.memset(t[:], 0.0))
            steps.done(pool.memset(ends[:, 0:1], 0.0))
            pool.sem_inc(consts, CONSTS - 1)
            pool.dma_start(heads2d(ks_out[0, 0])[0:KEEP - DEC, :], heads2d(cache_attn_k[0, 0])[DEC:KEEP, :]).then_inc(kv_out[0], 16)
            pool.dma_start(heads2d(vs_out[0, 0])[0:KEEP - DEC, :], heads2d(cache_attn_v[0, 0])[DEC:KEEP, :]).then_inc(kv_out[1], 16)
            attn_pool(pool)
            for l in range(LAYERS):
                scatter_pool(pool, l)
                gather_pool(pool, l)

        @block.scalar
        def _(act):
            steps = Steps(act, act_steps)
            act.wait_ge(consts, 1)
            norms_act(act, steps, 0)
            attn_act(act, steps)
            for l in range(LAYERS):
                if l == 1:
                    norms_act(act, steps, 2 * l)
                    conv_act(act, steps)
                norms_act(act, steps, 2 * l + 1)
                router_act(act, l)
                experts_act(act, l)
            norms_act(act, steps, 2 * LAYERS)

        @block.vector
        def _(dve):
            steps = Steps(dve, dve_steps)
            dve.wait_ge(rel_in, 16)
            V = nc.vector
            V.tensor_copy(rel_sb[0:HEADS, 0:P - 1], rel_sb[0:HEADS, P - 1:P].to_broadcast([HEADS, P - 1])).then_inc(rel_ext, 1)
            norms_dve(dve, steps, 0)
            dve.wait_ge(consts, CONSTS)
            attn_dve(dve, steps)
            project_dve(dve, steps, 0, None)
            for l in range(LAYERS):
                if l == 1:
                    norms_dve(dve, steps, 2 * l)
                    conv_dve(dve, steps)
                router_dve(dve, steps, l)
                experts_dve(dve, l)
            norms_dve(dve, steps, 2 * LAYERS)

        @block.tensor
        def _(pe):
            pe.wait_ge(ident0, 1)
            norms_pe(pe, 0)
            attn_pe(pe)
            pe.wait_ge(wo_in, 16)
            pe.wait_ge(op_ev, PAIRS + FREE)
            pe.wait_ge(os_ev, PAIRS)
            project_pe(pe, 0, ot, wo_sb, None)
            for l in range(LAYERS):
                if l == 1:
                    norms_pe(pe, 2 * l)
                    conv_pe(pe)
                experts_pe(pe, l)


_INS = ['x_prompt', 'x_sample', 'cache_attn_k', 'cache_attn_v', 'cache_conv', 'norm_mix', 'norm_ffn', 'norm_final',
        'w_qkv', 'w_o', 'rel_table', 'w_pw1', 'b_pw1', 'w_dw', 'b_dw', 'ln_g', 'ln_b', 'w_pw2', 'b_pw2',
        'w_group', 'b_group', 'w_router', 'b_router', 'w_gate', 'w_up', 'w_down']


def kernel(**inputs):
    import numpy as _np
    import concourse.bacc as _bacc
    from concourse.bass_utils import run_bass_kernel_spmd as _run

    shapes = {k: tuple(v.shape) for k, v in inputs.items()}
    kv = (shapes['cache_attn_k'][0], shapes['x_prompt'][0]) + shapes['cache_attn_k'][2:]
    conv = (shapes['cache_conv'][0], shapes['x_prompt'][0]) + shapes['cache_conv'][2:]
    outs = [shapes['x_prompt'], shapes['x_sample'], kv, kv, conv,
            shapes['cache_attn_k'], shapes['cache_attn_v'], shapes['cache_conv']]
    nc = _bacc.Bacc("TRN2", target_bir_lowering=False, num_devices=1)
    arrays, args = {}, []
    for name in _INS:
        a = _np.asarray(inputs[name])
        if name == 'rel_table':
            a = a[:, :, ::-1]
        a = _np.ascontiguousarray(a)
        arrays[f"in_{name}"] = a
        args.append(nc.dram_tensor(f"in_{name}", a.shape, mybir.dt.from_np(a.dtype), kind="ExternalInput").ap())
    for i, shape in enumerate(outs):
        args.append(nc.dram_tensor(f"out_{i}", shape, F32, kind="ExternalOutput").ap())
    encoder(nc, *args)
    r = _run(nc, [arrays], core_ids=[0])
    return tuple(r.results[0][f"out_{i}"] for i in range(len(outs)))
```
